# Optimizing a Trainium2 kernel written in Bass

```python
import jax, jax.numpy as jnp
from jax import lax
import numpy as np

D_MODEL = 1024
BATCH = 1
SEQ = 512
DEPTH = 2

HEAD_DIM = 64
N_HEADS = D_MODEL // HEAD_DIM
N_SB_HEADS = N_HEADS // 2
N_DIL_HEADS = N_HEADS - N_SB_HEADS
N_FOX_HEADS = N_HEADS
D_ATTN = N_HEADS * HEAD_DIM
D_FF = -(-8 * D_MODEL // (3 * 256)) * 256
ROPE_THETA = 500000.0
ROT_DIM = HEAD_DIM // 4
Q_BLOCK = 128
DIL_PATTERNS = ((128, 1), (512, 4), (2048, 16))
RMS_EPS = 1e-5
N_EVEN = (DEPTH + 1) // 2
N_ODD = DEPTH // 2

kernel_name = "hybrid_stickbreak_dilated_fox_trunk"

def rms_norm(x, g):
    xf = x.astype(jnp.float32)
    y = xf * lax.rsqrt(jnp.mean(xf * xf, axis=-1, keepdims=True) + RMS_EPS)
    return (y * g.astype(jnp.float32)).astype(x.dtype)

def partial_rotary(x, pos):
    half = ROT_DIM // 2
    inv_freq = ROPE_THETA ** (-jnp.arange(half, dtype=jnp.float32) * 2.0 / ROT_DIM)
    ang = pos[:, None] * inv_freq[None, :]
    cos = jnp.cos(ang)[:, None, :].astype(x.dtype)
    sin = jnp.sin(ang)[:, None, :].astype(x.dtype)
    x1, x2, x_pass = x[..., :half], x[..., half:ROT_DIM], x[..., ROT_DIM:]
    return jnp.concatenate([x1 * cos - x2 * sin, x2 * cos + x1 * sin, x_pass], axis=-1)

def stick_breaking_attention(q, k, v):
    B, H, S, Dh = q.shape
    nb = S // Q_BLOCK
    qb = q.reshape(B, H, nb, Q_BLOCK, Dh).transpose(2, 0, 1, 3, 4)
    kpos = jnp.arange(S)

    def block(args):
        qblk, n = args
        z = jnp.einsum('bhqd,bhkd->bhqk', qblk, k).astype(jnp.float32)
        qpos = n * Q_BLOCK + jnp.arange(Q_BLOCK)
        strict = kpos[None, :] < qpos[:, None]
        log_1m_beta = jnp.where(strict, jax.nn.log_sigmoid(-z), 0.0)
        between = lax.cumsum(log_1m_beta, axis=3, reverse=True) - log_1m_beta
        a = jnp.where(strict, jnp.exp(jax.nn.log_sigmoid(z) + between), 0.0)
        return jnp.einsum('bhqk,bhkd->bhqd', a.astype(v.dtype), v)

    out = lax.map(block, (qb, jnp.arange(nb)))
    return out.transpose(1, 2, 0, 3, 4).reshape(B, H, S, Dh)

def dilated_window_attention(q, k, v, window, dilation):
    B, S, H, Dh = q.shape
    span = window // dilation
    L = S // dilation
    nb = -(-L // span)
    Lp = nb * span

    def to_blocks(t):
        t = t.reshape(B, L, dilation, H, Dh)
        t = jnp.pad(t, ((0, 0), (0, Lp - L), (0, 0), (0, 0), (0, 0)))
        return t.reshape(B, nb, span, dilation, H, Dh)

    def with_prev(t):
        prev = jnp.pad(t[:, :-1], ((0, 0), (1, 0), (0, 0), (0, 0), (0, 0), (0, 0)))
        return jnp.concatenate([prev, t], axis=2)

    qb = to_blocks(q)
    kw = with_prev(to_blocks(k))
    vw = with_prev(to_blocks(v))
    s = jnp.einsum('bnqrhd,bnkrhd->bnrhqk', qb, kw).astype(jnp.float32)
    a = jnp.arange(span)[None, :, None]
    kk = jnp.arange(2 * span)[None, None, :]
    blk = jnp.arange(nb)[:, None, None]
    valid = (kk >= a) & (kk <= a + span) & (blk * span - span + kk >= 0)
    s = jnp.where(valid[None, :, None, None], s, -jnp.inf)
    m = jnp.max(s, axis=-1, keepdims=True)
    p = jnp.exp(s - m)
    l = jnp.sum(p, axis=-1, keepdims=True)
    o = jnp.einsum('bnrhqk,bnkrhd->bnqrhd', (p / l).astype(v.dtype), vw)
    lse = (m + jnp.log(l))[..., 0]
    o = o.reshape(B, Lp, dilation, H, Dh)[:, :L].reshape(B, S, H, Dh)
    lse = lse.transpose(0, 1, 4, 2, 3).reshape(B, Lp, dilation, H)[:, :L].reshape(B, S, H)
    return o, lse

def forgetting_attention(q, k, v, log_f):
    B, H, S, Dh = q.shape
    F = lax.cumsum(log_f, axis=2)
    nb = S // Q_BLOCK
    qb = q.reshape(B, H, nb, Q_BLOCK, Dh).transpose(2, 0, 1, 3, 4)
    Fb = F.reshape(B, H, nb, Q_BLOCK).transpose(2, 0, 1, 3)
    kpos = jnp.arange(S)

    def block(args):
        qblk, Fq, n = args
        z = jnp.einsum('bhqd,bhkd->bhqk', qblk, k).astype(jnp.float32)
        z = z + Fq[..., None] - F[:, :, None, :]
        qpos = n * Q_BLOCK + jnp.arange(Q_BLOCK)
        z = jnp.where(kpos[None, :] <= qpos[:, None], z, -jnp.inf)
        p = jax.nn.softmax(z, axis=-1)
        return jnp.einsum('bhqk,bhkd->bhqd', p.astype(v.dtype), v)

    out = lax.map(block, (qb, Fb, jnp.arange(nb)))
    return out.transpose(1, 2, 0, 3, 4).reshape(B, H, S, Dh)

def even_mixer(h, w_qkv, w_o):
    B, S, _ = h.shape
    scale = HEAD_DIM ** -0.5
    qkv = (h @ w_qkv).reshape(B, S, 3, N_HEADS, HEAD_DIM)
    q, k, v = qkv[:, :, 0], qkv[:, :, 1], qkv[:, :, 2]
    qa = (q[:, :, :N_SB_HEADS] * scale).transpose(0, 2, 1, 3)
    ka = k[:, :, :N_SB_HEADS].transpose(0, 2, 1, 3)
    va = v[:, :, :N_SB_HEADS].transpose(0, 2, 1, 3)
    out_a = stick_breaking_attention(qa, ka, va).transpose(0, 2, 1, 3)
    pos = jnp.arange(S, dtype=jnp.float32)
    qd = partial_rotary(q[:, :, N_SB_HEADS:], pos) * scale
    kd = partial_rotary(k[:, :, N_SB_HEADS:], pos)
    vd = v[:, :, N_SB_HEADS:]
    outs, lses = [], []
    for window, dilation in DIL_PATTERNS:
        o_p, lse_p = dilated_window_attention(qd, kd, vd, window, dilation)
        outs.append(o_p)
        lses.append(lse_p)
    mix = jax.nn.softmax(jnp.stack(lses), axis=0)
    out_b = jnp.einsum('pbsh,pbshd->bshd', mix.astype(vd.dtype), jnp.stack(outs))
    o = jnp.concatenate([out_a, out_b], axis=2).reshape(B, S, D_ATTN)
    return o @ w_o

def odd_mixer(h, w_qkvf, b_forget, w_o):
    B, S, _ = h.shape
    scale = HEAD_DIM ** -0.5
    proj = h @ w_qkvf
    qkv = proj[..., :3 * D_ATTN].reshape(B, S, 3, N_FOX_HEADS, HEAD_DIM)
    f_logit = proj[..., 3 * D_ATTN:] + b_forget
    log_f = jax.nn.log_sigmoid(f_logit.astype(jnp.float32)).transpose(0, 2, 1)
    q = (qkv[:, :, 0] * scale).transpose(0, 2, 1, 3)
    k = qkv[:, :, 1].transpose(0, 2, 1, 3)
    v = qkv[:, :, 2].transpose(0, 2, 1, 3)
    o = forgetting_attention(q, k, v, log_f).transpose(0, 2, 1, 3).reshape(B, S, D_ATTN)
    return o @ w_o

def swiglu(h, w_in, w_out):
    g, u = jnp.split(h @ w_in, 2, axis=-1)
    return (jax.nn.silu(g) * u) @ w_out

def setup_inputs(seed: int = 0) -> dict:
    key = jax.random.key(seed)
    ks = jax.random.split(key, 12)
    f32 = jnp.float32
    res_scale = (2.0 * DEPTH) ** -0.5
    x = jax.random.normal(ks[0], (BATCH, SEQ, D_MODEL), f32)
    norm_mix = 1.0 + 0.02 * jax.random.normal(ks[1], (DEPTH, D_MODEL), f32)
    w_qkv_even = jax.random.normal(ks[2], (N_EVEN, D_MODEL, 3 * D_ATTN), f32) * D_MODEL ** -0.5
    w_o_even = jax.random.normal(ks[3], (N_EVEN, D_ATTN, D_MODEL), f32) * (D_ATTN ** -0.5 * res_scale)
    w_qkvf_odd = jax.random.normal(ks[4], (N_ODD, D_MODEL, 3 * D_ATTN + N_FOX_HEADS), f32) * D_MODEL ** -0.5
    b_forget = jax.random.uniform(ks[5], (N_ODD, N_FOX_HEADS), f32, minval=1.0, maxval=4.0)
    w_o_odd = jax.random.normal(ks[6], (N_ODD, D_ATTN, D_MODEL), f32) * (D_ATTN ** -0.5 * res_scale)
    norm_ffn = 1.0 + 0.02 * jax.random.normal(ks[7], (DEPTH, D_MODEL), f32)
    w_ffn_in = jax.random.normal(ks[8], (DEPTH, D_MODEL, 2 * D_FF), f32) * D_MODEL ** -0.5
    w_ffn_out = jax.random.normal(ks[9], (DEPTH, D_FF, D_MODEL), f32) * (D_FF ** -0.5 * res_scale)
    norm_final = 1.0 + 0.02 * jax.random.normal(ks[10], (D_MODEL,), f32)
    return {"x": x, "norm_mix": norm_mix, "w_qkv_even": w_qkv_even, "w_o_even": w_o_even,
            "w_qkvf_odd": w_qkvf_odd, "b_forget": b_forget, "w_o_odd": w_o_odd,
            "norm_ffn": norm_ffn, "w_ffn_in": w_ffn_in, "w_ffn_out": w_ffn_out,
            "norm_final": norm_final}

def reference(x, norm_mix, w_qkv_even, w_o_even, w_qkvf_odd, b_forget, w_o_odd,
              norm_ffn, w_ffn_in, w_ffn_out, norm_final):
    for layer in range(DEPTH):
        h = rms_norm(x, norm_mix[layer])
        if layer % 2 == 0:
            x = x + even_mixer(h, w_qkv_even[layer // 2], w_o_even[layer // 2])
        else:
            x = x + odd_mixer(h, w_qkvf_odd[layer // 2], b_forget[layer // 2], w_o_odd[layer // 2])
        h = rms_norm(x, norm_ffn[layer])
        x = x + swiglu(h, w_ffn_in[layer], w_ffn_out[layer])
    return rms_norm(x, norm_final)


_drawn_inputs = setup_inputs


def setup_inputs(seed=0):
    import zlib

    import numpy as np

    out = dict(_drawn_inputs(seed))
    spreads = {}
    factors = {'norm_mix': 6.966, 'norm_ffn': 4.958, 'norm_final': 2.922}
    for name, (base, spread) in spreads.items():
        noise = np.random.default_rng([zlib.crc32(name.encode()), seed]).standard_normal(out[name].shape)
        drawn = base * np.exp(spread * noise) if base else spread * noise
        out[name] = __import__('jax').numpy.asarray(drawn.astype(out[name].dtype))
    for name, factor in factors.items():
        out[name] = (out[name] * factor).astype(out[name].dtype)
    return out
```

```python
from contextlib import ExitStack

import numpy as np
import concourse.bass as bass
from concourse import mybir

F32 = mybir.dt.float32
F32R = mybir.dt.float32r
BF16 = mybir.dt.bfloat16
ALU = mybir.AluOpType
ACT = mybir.ActivationFunctionType
AX = mybir.AxisListType.X

P = 128
D, T, DH, DFF, DEPTH = 1024, 512, 64, 2816, 2
NB = D // P
NT = T // P
NF = DFF // P
NPAIR = D // (2 * DH)
HEADS = 2 * NPAIR
STICK = NPAIR // 2
SCALE = DH ** -0.5
EPS = 1e-5
THETA = 500000.0
ROT = DH // 4
CONSTS = 7
MASKED = -1e30
LINEAR = 30.0
JOB = 8 * P

KW = [T - b * P for b in range(NT)]
KO = [sum(KW[:b]) for b in range(NT)]
QW = [(b + 1) * P for b in range(NT)]
QO = [sum(QW[:b]) for b in range(NT)]
TRI = sum(KW)

JV, JQK, JO, JIN, NOUT = 8, 2 * NPAIR, NB, 2 * NF, 3
OUT_CHUNKS = [(0, 8), (8, 15), (15, 22)]
JATT = [JV + JQK + JO, JV + 1 + JQK + JO]
JOB0 = [0, JATT[0] + JIN + NOUT * NB]
SWAP = [(i + ROT // 2) % ROT if i < ROT else i for i in range(32)]


def loop(eng, start, end, body):
    if end - start == 1:
        body(start)
    elif end > start:
        with eng.Fori(start, end) as i:
            body(i)


def blk(i):
    return bass.ds(i, 1)


def trunk(nc, xt_d, gains_d, wa0_d, wa1_d, wf_d, win_d, wout_d, bf_d, rope_d, mult_d, masks_d, out_d):
    ctx = ExitStack()
    with ctx:
        def sb(name, shape, dt=F32):
            return ctx.enter_context(nc.sbuf_tensor(name, shape, dt))

        def bank(name):
            return ctx.enter_context(nc.psum_tensor(name, [P, T], F32))

        def sem(name):
            return ctx.enter_context(nc.semaphore(name))

        x = sb("x", [P, NB, T])
        h_hi = sb("h_hi", [P, NB, T], F32R)
        h_lo = sb("h_lo", [P, NB, T], F32R)
        w_raw = sb("w_raw", [P, 2, JOB])
        w_hi = sb("w_hi", [P, 2, JOB], F32R)
        w_lo = sb("w_lo", [P, 2, JOB], F32R)
        f_hi = sb("f_hi", [P, NF * T], F32R)
        f_lo = sb("f_lo", [P, NF * T], F32R)

        used = [0]

        def parts(n, *shape):
            a, used[0] = used[0], used[0] + n
            assert used[0] <= NF * T
            return f_hi[:, a:a + n], f_lo[:, a:a + n]

        o_hi, o_lo = (v.rearrange("p (c t) -> p c t", c=NB) for v in parts(NB * T))
        pt = [parts(TRI) for _ in range(2)]
        sp_hi, sp_lo = parts(TRI)
        q_hi, q_lo = parts(T)
        k_hi, k_lo = parts(T)
        v_hi, v_lo = (v.rearrange("p (c t) -> p c t", c=NT) for v in parts(NT * P))
        fa, fb = (v.rearrange("p (c t) -> p c t", c=2) for v in parts(2 * T))
        neg_tri, neg_one = parts(P)

        v32 = sb("v32", [P, NT, D])
        s32 = [sb(f"s32_{i}", [P, TRI]) for i in range(2)]
        tmp = sb("tmp", [P, T])
        tmp2 = sb("tmp2", [P, T])
        rms = sb("rms", [P, T])
        rms_col = sb("rms_col", [P, NT])
        cosr = sb("cosr", [P, T])
        sinr = sb("sinr", [P, T])
        mult = sb("mult", [P, T])
        ssq = sb("ssq", [P, T])
        ones = sb("ones", [P, P])
        ident = sb("ident", [P, P])
        ident_b = sb("ident_b", [P, P], BF16)
        m_dil = sb("m_dil", [P, T], BF16)
        m_causal = sb("m_causal", [P, P], BF16)
        m_strict = sb("m_strict", [P, P], BF16)
        gains = sb("gains", [P, 2 * DEPTH + 1, NB])
        bforget = sb("bforget", [HEADS, 1])
        eps = sb("eps", [P, 1])
        nmax = sb("nmax", [P, NT])
        rsum = sb("rsum", [P, NT])
        rinv = sb("rinv", [P, NT])
        f_rows = nc.dram_tensor("f_rows", (2, 4, HEADS, T), F32).ap()
        masks32 = v32[:, 0, :]

        zb = [bank(f"zb{b}") for b in range(NT)]
        pb = [bank(f"pb{b}") for b in range(2)]
        ob = [bank(f"ob{b}") for b in range(2)]
        vb = [zb, [ob[0], ob[1], pb[0], pb[1]]]

        x_loaded = [sem(f"x_loaded{i}") for i in range(4)]
        gains_loaded, const_loaded, const_ready, ones_ready = (sem(n) for n in ("gains_loaded", "const_loaded", "const_ready", "ones_ready"))
        w_loaded = [sem("w_loaded0"), sem("w_loaded1")]
        w_hi_ready, w_lo_ready, job_done = sem("w_hi_ready"), sem("w_lo_ready"), sem("job_done")
        h_hi_ready, h_lo_ready, x_new = sem("h_hi_ready"), sem("h_lo_ready"), sem("x_new")
        sq_ready, ssq_ready, ssq_summed, ln_done, rms_ready = (sem(n) for n in ("sq_ready", "ssq_ready", "ssq_summed", "ln_done", "rms_ready"))
        v_ready = sem("v_ready")
        qk_scaled, qk_hi_ready, qk_ready = (sem(n) for n in ("qk_scaled", "qk_hi_ready", "qk_ready"))
        vs_hi_ready, vs_ready = sem("vs_hi_ready"), sem("vs_ready")
        z_ready, min_ready, exp_done, ln_ready = (sem(n) for n in ("z_ready", "min_ready", "exp_done", "ln_ready"))
        sp_ready, sp_hi_ready, sp_lo_ready = sem("sp_ready"), sem("sp_hi_ready"), sem("sp_lo_ready")
        max_ready, rows_exp, rows_mult, rows_inv, rows_ready = (sem(n) for n in ("max_ready", "rows_exp", "rows_mult", "rows_inv", "rows_ready"))
        second_ready, stick_exp, pt_hi_ready, pt_lo_ready = (sem(n) for n in ("second_ready", "stick_exp", "pt_hi_ready", "pt_lo_ready"))
        o_summed, o_hi_ready, o_lo_ready = sem("o_summed"), sem("o_hi_ready"), sem("o_lo_ready")
        g_scaled, g_sig, g_silu, u_scaled, act_ready, f_hi_ready, f_lo_ready = (sem(n) for n in (
            "g_scaled", "g_sig", "g_silu", "u_scaled", "act_ready", "f_hi_ready", "f_lo_ready"))
        fg_step, fg_act, rows_stored, rows_loaded = (sem(n) for n in ("fg_step", "fg_act", "rows_stored", "rows_loaded"))
        eps_ready, col_ready = sem("eps_ready"), sem("col_ready")
        rope_ready, rope_step, out_ready, out_stored = sem("rope_ready"), sem("rope_step"), sem("out_ready"), sem("out_stored")

        f_gate, f_sig, f_silu, f_up = s32[0][:, 0:T], s32[0][:, T:2 * T], s32[1][:, 0:T], s32[1][:, T:2 * T]
        fg_z, fg_soft, fg_sum, fg_one = (v[0:HEADS, :] for v in (f_gate, f_sig, f_silu, f_up))
        y32 = v32[:].rearrange("p a b -> p (a b)").rearrange("p (m t) -> p m t", m=NB)
        g_job = JOB0[1] + JV

        def gate_cols(w):
            return w[:, g_job % 2, :].rearrange("p (c n) -> p c n", c=NB)[:, :, 0:HEADS]

        tmp_r = [v[0:HEADS, :] for v in (sp_hi[:, 0:T], sp_hi[:, T:2 * T], sp_lo[:, 0:T], sp_lo[:, T:2 * T], pt[1][0][:, 0:T])]

        block = ctx.enter_context(nc.Block())

        def first_qk_job(L):
            return JOB0[L] + JV + L

        def out_job(L):
            return JOB0[L] + JATT[L] - JO

        def ffn_job(L):
            return JOB0[L] + JATT[L]

        def ffn_out_job(L):
            return ffn_job(L) + JIN

        @block.sync
        def _(sp):
            def load(n0, di, half, src, width=JOB):
                s = n0 % 2
                if n0 >= 2:
                    sp.wait_ge(w_hi_ready, di + (n0 - 1))
                    sp.wait_ge(w_lo_ready, di + (n0 - 1))
                sp.dma_start(w_raw[:, s, 0:width], src).then_inc(w_loaded[s], 16)

            def loads(n0, count, dram, first):
                def two(i):
                    for e in range(2):
                        load(n0 + e, i * 2, i, dram[blk(i * 2 + (first + e))].rearrange("o p n -> p (o n)"))
                loop(sp, 0, count // 2, two)

            sp.dma_start(gains[:], gains_d).then_inc(gains_loaded, 16)
            for i in range(4):
                sp.dma_start(x[:, 2 * i:2 * i + 2, :], xt_d[:, 2 * i:2 * i + 2, :]).then_inc(x_loaded[i], 16)
                if i < 2:
                    load(i, 0, 0, wa0_d[i])
            sp.dma_start(masks32, masks_d).then_inc(const_loaded, 16)
            sp.dma_start(cosr[:], rope_d[0]).then_inc(const_loaded, 16)
            sp.dma_start(sinr[:], rope_d[1]).then_inc(const_loaded, 16)
            sp.dma_start(mult[:], mult_d).then_inc(const_loaded, 16)
            sp.dma_start(bforget[:], bf_d).then_inc(const_loaded, 16)

            def f_load(j):
                for ab, rows in enumerate((fa, fb)):
                    sp.dma_start(rows[0:4, :, :].bitcast(F32), f_rows[ab][:, bass.ds(j * 2, 2), :]).then_inc(rows_loaded, 16)

            for L in range(DEPTH):
                n = JOB0[L]
                wa = (wa0_d, wa1_d)[L]
                if L == 0:
                    loads(2, JATT[0] - 2, wa, 2)
                else:
                    loads(n, JV, wa, 0)
                    g = n + JV
                    sp.wait_ge(w_hi_ready, g - 1)
                    sp.wait_ge(w_lo_ready, g - 1)
                    sp.dma_start(w_raw[:, g % 2, :].rearrange("p (c n) -> p c n", c=NB)[:, :, 0:HEADS], wf_d).then_inc(w_loaded[g % 2], 16)
                    loads(n + JV + 1, 2, wa, JV)
                    sp.wait_ge(fg_step, 7)
                    sp.wait_ge(fg_act, 5)
                    one, hi, lo, nhi, nlo = (tmp_r[i] for i in range(5))
                    for ab, rows in enumerate(((one, one, hi, lo), (nhi, nlo, one, one))):
                        for r, src in enumerate(rows):
                            sp.dma_start(f_rows[ab, r], src.bitcast(F32)).then_inc(rows_stored, 16)
                    sp.wait_ge(rows_stored, 16 * 8)
                    f_load(0)

                    def pair(j):
                        for e in range(2):
                            load(n + JV + 3 + e, j * 2, j, wa[blk(j * 2 + (JV + 2 + e))].rearrange("o p n -> p (o n)"))
                        sp.wait_ge(z_ready, j * (2 * NT) + (HEADS + 2) * NT)
                        f_load(j + 1)
                    loop(sp, 0, NPAIR - 1, pair)
                    loads(n + JV + 1 + JQK, JO, wa, JV + JQK)
                loads(ffn_job(L), JIN, win_d[L], 0)
                no = ffn_out_job(L)

                def two_tiles(i):
                    for e in range(2):
                        for c, (a, b) in enumerate(OUT_CHUNKS):
                            k = NOUT * e + c
                            load(no + k, i * 6, i * 3,
                                 wout_d[L][blk(i * 2 + e), :, a * P:b * P].rearrange("o p n -> p (o n)"), (b - a) * P)
                loop(sp, 0, NB // 2, two_tiles)

            for m in range(NB):
                sp.wait_ge(out_ready, m + 1)
                sp.dma_start(out_d[:, m, :], v32[:].rearrange("p a b -> p (a b)")[:, m * T:(m + 1) * T]).then_inc(out_stored, 16)
            sp.wait_ge(out_stored, 16 * NB)


        @block.tensor
        def _(pe):
            mm = nc.tensor.matmul

            def job_ready(n0, di):
                pe.wait_ge(w_hi_ready, di + (n0 + 1))
                pe.wait_ge(w_lo_ready, di + (n0 + 1))

            def product(out, s, chunks, hi, lo, start=True, stop=True, wait=None):
                for c, k in enumerate(chunks):
                    if wait:
                        wait(k)
                    wh, wl = w_hi[:, s, c * P:(c + 1) * P], w_lo[:, s, c * P:(c + 1) * P]
                    mm(out, wh, hi[:, k, :], start=start and c == 0, stop=False)
                    mm(out, wh, lo[:, k, :], start=False, stop=False)
                    last = mm(out, wl, hi[:, k, :], start=False, stop=stop and c == len(chunks) - 1)
                last.then_inc(job_done, 1)

            def h_ready(stage):
                def wait(k):
                    pe.wait_ge(h_hi_ready, stage * NB + k + 1)
                    pe.wait_ge(h_lo_ready, stage * NB + k + 1)
                return wait

            def sum_squares(stage, cols):
                pe.wait_ge(ssq_ready, (stage + 1) * NB)
                if stage:
                    pe.wait_ge(x_new, stage * NB)
                last = mm(pb[0][:], ones[:], ssq[:], start=True, stop=True)
                if cols:
                    for t in range(NT):
                        last = mm(pb[1][:, t:t + 1], ssq[:, t * P:(t + 1) * P], ones[:, 0:1], start=True, stop=True)
                last.then_inc(ssq_summed, 1)

            def scores(kind, e):
                r = slice(DH * e, DH * (e + 1))
                for b in (range(NT) if kind != "stick" else reversed(range(NT))):
                    own = slice(b * P, (b + 1) * P)
                    if kind == "stick":
                        w, st, mv, move = KW[b], (k_hi, k_lo), (q_hi, q_lo), slice(b * P, T)
                        mask, at = m_strict[:], slice(0, P)
                    else:
                        w, st, mv, move = QW[b], (q_hi, q_lo), (k_hi, k_lo), slice(0, QW[b])
                        mask, at = (m_dil[:, T - w:T], slice(0, w)) if kind == "dil" else (m_causal[:], slice(w - P, w))
                    out = zb[b][:, 0:w]
                    mm(out, st[0][r, own], mv[0][r, move], start=True, stop=False)
                    mm(out, st[0][r, own], mv[1][r, move], start=False, stop=False)
                    mm(out, st[1][r, own], mv[0][r, move], start=False, stop=False)
                    if kind == "fox":
                        mm(out, fa[0:4, e, own], fb[0:4, e, move], start=False, stop=False)
                    mm(zb[b][:, at], ident_b[:], mask, start=False, stop=True).then_inc(z_ready, 1)

            def suffix_sums(S):
                for n, b in enumerate(reversed(range(NT))):
                    pe.wait_ge(sp_hi_ready, S * NT + (n + 1))
                    pe.wait_ge(sp_lo_ready, S * NT + (n + 1))
                    for later in range(b + 1, NT):
                        for v in (sp_hi, sp_lo):
                            mm(zb[b][:, (later - b) * P:KW[b]], neg_one, v[:, KO[later]:KO[later] + KW[later]],
                               start=False, stop=False, skip_group_check=True)
                    for v in (sp_hi, sp_lo):
                        last = mm(zb[b][:, 0:KW[b]], neg_tri, v[:, KO[b]:KO[b] + KW[b]],
                                  start=False, stop=v is sp_lo, skip_group_check=True)
                    last.then_inc(second_ready, 1)

            def transposes(X, e):
                for b in range(NT):
                    pe.wait_ge(rows_ready, X * NT + (b + 1))
                    for k in range(b + 1):
                        last = nc.tensor.transpose(zb[k][:, (b - k) * P:(b - k + 1) * P],
                                                   s32[e][:, QO[b] + k * P:QO[b] + (k + 1) * P], ident[:])
                        if b == NT - 1:
                            last.then_inc(second_ready, 1)

            def values(S, e):
                pe.wait_ge(pt_hi_ready, S * NT + NT)
                pe.wait_ge(pt_lo_ready, S * NT + NT)
                hi, lo = pt[e]
                for b in range(NT):
                    out, c = ob[e][:, b * P:T], slice(KO[b], KO[b] + KW[b])
                    mm(out, v_hi[:, b, :], hi[:, c], start=b == 0, stop=False)
                    mm(out, v_hi[:, b, :], lo[:, c], start=False, stop=False)
                    last = mm(out, v_lo[:, b, :], hi[:, c], start=False, stop=b == NT - 1)
                last.then_inc(o_summed, 1)

            def pair(L, kind, j, first=False, last_pair=False):
                for e in range(2):
                    S = j * 2 + (L * HEADS + e)
                    pe.wait_ge(qk_ready, j * 2 + (L * HEADS + 2))
                    if not (L == 0 and first and e == 0):
                        pe.wait_ge(pt_hi_ready, S * NT)
                        pe.wait_ge(pt_lo_ready, S * NT)
                    if kind == "fox":
                        pe.wait_ge(rows_loaded, j * 32 + 32)
                    scores(kind, e)
                    if not last_pair:
                        n0 = first_qk_job(L) + 2 + e
                        job_ready(n0, j * 2)
                        product(pb[e][:], n0 % 2, range(NB), h_hi, h_lo)
                    if kind == "stick":
                        suffix_sums(S)
                    else:
                        transposes(S - 2 * STICK, e)
                    if not (first and e == 0):
                        if not first:
                            pe.wait_ge(o_hi_ready, S - 1)
                            pe.wait_ge(o_lo_ready, S - 1)
                        if e == 1:
                            pe.wait_ge(vs_ready, j + (L * NPAIR + 1))
                        values(S - 1, 1 - e)

            pe.wait_ge(const_ready, CONSTS)
            pe.wait_ge(ones_ready, 1)
            for L in range(DEPTH):
                stage = 2 * L
                n = JOB0[L]
                for half in range(2):
                    for c2 in range(4):
                        job = n + 4 * half + c2
                        job_ready(job, 0)
                        s = job % 2
                        for c in range(2):
                            k = 2 * c2 + c
                            if half == 0:
                                h_ready(stage)(k)
                            wh, wl = w_hi[:, s, c * T:(c + 1) * T], w_lo[:, s, c * T:(c + 1) * T]
                            for t in range(NT):
                                out, tt = vb[half][t][:], slice(t * P, (t + 1) * P)
                                if half == 1 and k == 0 and t == 2:
                                    pe.wait_ge(rms_ready, stage + 1)
                                mm(out, h_hi[:, k, tt], wh, start=k == 0, stop=False)
                                mm(out, h_hi[:, k, tt], wl, start=False, stop=False)
                                last = mm(out, h_lo[:, k, tt], wh, start=False, stop=k == NB - 1)
                        last.then_inc(job_done, 1)
                    if half == 0:
                        sum_squares(stage, True)
                pe.wait_ge(v_ready, (2 * L + 1) * NT)
                if L == 1:
                    job_ready(n + JV, 0)
                    product(zb[0][:], (n + JV) % 2, range(NB), h_hi, h_lo)
                pe.wait_ge(v_ready, (2 * L + 2) * NT)
                for e in range(2):
                    n0 = first_qk_job(L) + e
                    job_ready(n0, 0)
                    product(pb[e][:], n0 % 2, range(NB), h_hi, h_lo)
                if L == 0:
                    pair(0, "stick", 0, first=True)
                    loop(pe, 1, STICK, lambda j: pair(0, "stick", j))
                    loop(pe, STICK, NPAIR - 1, lambda j: pair(0, "dil", j))
                    pair(0, "dil", NPAIR - 1, last_pair=True)
                else:
                    pe.wait_ge(fg_step, 1)
                    pair(1, "fox", 0, first=True)
                    loop(pe, 1, NPAIR - 1, lambda j: pair(1, "fox", j))
                    pair(1, "fox", NPAIR - 1, last_pair=True)
                S = (L + 1) * HEADS
                pe.wait_ge(o_hi_ready, S - 2)
                pe.wait_ge(o_lo_ready, S - 2)
                values(S - 1, 1)

                def added(stage, i, e):
                    pe.wait_ge(x_new, i * 2 + ((stage - 1) * NB + e - 1))

                pe.wait_ge(o_hi_ready, S)
                pe.wait_ge(o_lo_ready, S)
                nj = out_job(L)

                def out_tiles(i, first=False):
                    for e in range(2):
                        if not first:
                            added(stage + 1, i, e)
                        job_ready(nj + e, i * 2)
                        product(pb[e][:], (nj + e) % 2, range(NB), o_hi, o_lo)
                out_tiles(0, first=True)
                loop(pe, 1, NB // 2, out_tiles)

                nj = ffn_job(L)

                def in_tile(i, first=False):
                    if not first:
                        pe.wait_ge(g_scaled, i + L * NF)
                    job_ready(nj, i * 2)
                    product(zb[0][:], nj % 2, range(NB), h_hi, h_lo, wait=h_ready(stage + 1) if first else None)
                    if first:
                        sum_squares(stage + 1, False)
                    else:
                        pe.wait_ge(u_scaled, i + L * NF)
                    job_ready(nj + 1, i * 2)
                    product(zb[1][:], (nj + 1) % 2, range(NB), h_hi, h_lo)
                in_tile(0, first=True)
                loop(pe, 1, NF, in_tile)

                nj = ffn_out_job(L)
                fh = f_hi[:].rearrange("p (c t) -> p c t", c=NF)
                fl = f_lo[:].rearrange("p (c t) -> p c t", c=NF)

                def f_ready(k):
                    pe.wait_ge(f_hi_ready, L * NF + k + 1)
                    pe.wait_ge(f_lo_ready, L * NF + k + 1)

                def ffn_tiles(i, first=False):
                    for e in range(2):
                        if not first:
                            added(stage + 2, i, e)
                        for c, (a, b) in enumerate(OUT_CHUNKS):
                            k = NOUT * e + c
                            job_ready(nj + k, i * 6)
                            product(pb[e][:], (nj + k) % 2, range(a, b), fh, fl, c == 0, c == NOUT - 1,
                                    f_ready if first and e == 0 else None)
                ffn_tiles(0, first=True)
                loop(pe, 1, NB // 2, ffn_tiles)
            sum_squares(2 * DEPTH, False)

        @block.scalar
        def _(act):
            f = nc.scalar.activation

            def alone():
                nc.scalar.nop(nofuse=True)

            def split(n0, di=0, half=0, width=JOB, view=None):
                s = n0 % 2
                act.wait_ge(w_loaded[s], half * 16 + 16 * (n0 // 2 + 1))
                if n0 >= 2:
                    act.wait_ge(job_done, di + (n0 - 1))
                view = view or (lambda w: w[:, s, 0:width])
                f(view(w_hi), view(w_raw), ACT.Copy).then_inc(w_hi_ready, 1)

            def squares(stage, m, e, first=False):
                if not first:
                    act.wait_ge(ssq_ready, m + (stage * NB - 1))
                    alone()
                f((tmp, tmp2)[e][:], x[:, m if isinstance(m, slice) else blk(m), :], ACT.Square).then_inc(sq_ready, 1)

            def gained(stage, m, e):
                g = gains[:, stage, blk(m)]
                if stage < 2 * DEPTH:
                    f(h_hi[:, blk(m), :], x[:, blk(m), :], ACT.Copy, scale=g).then_inc(h_hi_ready, 1)
                else:
                    f(y32[:, blk(m), :], x[:, blk(m), :], ACT.Copy, scale=g).then_inc(h_hi_ready, 1)

            def inverse_rms(stage, cols, lns):
                act.wait_ge(ssq_summed, stage + 1)
                f(rms[:], pb[0][:], ACT.Ln, bias=eps[:], scale=1.0 / D).then_inc(ln_done, 1)
                if cols:
                    f(rms_col[:], pb[1][:, 0:NT], ACT.Ln, bias=eps[:], scale=1.0 / D).then_inc(ln_done, 1)
                    act.wait_ge(ln_done, lns + 2)
                    f(rms_col[:], rms_col[:], ACT.Exp, scale=-0.5).then_inc(col_ready, 1)
                act.wait_ge(ln_done, lns + 1)
                f(rms[:], rms[:], ACT.Exp, scale=-0.5).then_inc(rms_ready, 1)

            def heads_out(S, e, at):
                act.wait_ge(o_summed, S + 1)
                alone()
                r = slice(DH * e, DH * (e + 1))
                f(o_hi[r, at, :], ob[e][r, :], ACT.Copy).then_inc(o_hi_ready, 1)

            def pair(L, kind, j, first=False, last_pair=False):
                for e in range(2):
                    S = j * 2 + (L * HEADS + e)
                    buf = s32[e]
                    if kind == "stick":
                        for n, b in enumerate(reversed(range(NT))):
                            act.wait_ge(min_ready, S * NT + (n + 1))
                            c = slice(KO[b], KO[b] + KW[b])
                            f(buf[:, c], buf[:, c], ACT.Exp).then_inc(exp_done, 1)
                        for n, b in enumerate(reversed(range(NT))):
                            act.wait_ge(exp_done, S * NT + (n + 1))
                            c = slice(KO[b], KO[b] + KW[b])
                            f(buf[:, c], buf[:, c], ACT.Ln, bias=1.0).then_inc(ln_ready, 1)
                    else:
                        X = S - 2 * STICK
                        for b in range(NT):
                            act.wait_ge(max_ready, X * NT + (b + 1))
                            sums = {"accum_out": rsum[:, b:b + 1]} if kind == "fox" else {}
                            f(buf[:, QO[b]:QO[b] + QW[b]], zb[b][:, 0:QW[b]], ACT.Exp,
                              bias=nmax[:, b:b + 1], **sums).then_inc(rows_exp, 1)
                    if not last_pair:
                        split(first_qk_job(L) + 3 + e, j * 2, j)
                    if not first:
                        heads_out(S - 2, e, blk(j - 1))
                    if e == 1:
                        f(v_hi[:], v32[:, :, bass.ds(j * P, P)], ACT.Copy).then_inc(vs_hi_ready, 1)
                    if kind == "stick":
                        for n, b in enumerate(reversed(range(NT))):
                            act.wait_ge(second_ready, S * NT + (n + 1))
                            f(buf[:, KO[b]:KO[b] + KW[b]], zb[b][:, 0:KW[b]], ACT.Exp).then_inc(stick_exp, 1)
                    else:
                        for b in range(NT):
                            act.wait_ge(second_ready, S * NT + (b + 1))
                            f(pt[e][0][:, KO[b]:KO[b] + KW[b]], zb[b][:, 0:KW[b]], ACT.Copy).then_inc(pt_hi_ready, 1)

            nc.scalar.preload_act_table_set("natural_log_exp_and_others")
            act.wait_ge(gains_loaded, 16)
            act.wait_ge(eps_ready, 1)
            for m in range(NB):
                act.wait_ge(x_loaded[m // 2], 16)
                gained(0, m, m % 2)
                squares(0, m, m % 2, first=m < 2)
                if m < 2:
                    split(m)
            act.wait_ge(const_loaded, 16 * 5)
            act.wait_ge(ones_ready, 1)
            for dst, a, b in ((m_dil[:], 0, T), (m_causal[:], T, T + P), (m_strict[:], T + P, T + 2 * P),
                              (ident_b[:], T + 2 * P, T + 3 * P), (ident[:], T + 2 * P, T + 3 * P), (neg_tri, T + 3 * P, D)):
                f(dst, masks32[:, a:b], ACT.Copy).then_inc(const_ready, 1)
            f(neg_one, ones[:], ACT.Copy, scale=-1.0).then_inc(const_ready, 1)

            for L in range(DEPTH):
                stage = 2 * L
                n = JOB0[L]
                last_v = n + JV - 1
                if L == 1:
                    nc.scalar.preload_act_table_set("natural_log_exp_and_others")
                for c in range(JV):
                    if c == 4:
                        inverse_rms(stage, True, 3 * L)
                        act.wait_ge(col_ready, L + 1)
                        act.wait_ge(job_done, n + 4)
                        for t in range(NT):
                            f(v32[:, t, 0:T], zb[t][:], ACT.Copy, scale=rms_col[:, t:t + 1]).then_inc(v_ready, 1)
                        continue
                    if c > 0 or L > 0:
                        if n + c + 1 > last_v and L == 1:
                            split(g_job, view=gate_cols)
                        else:
                            split(n + c + 1)
                    if c == 3:
                        split(n + 5)
                fq = first_qk_job(L)
                if L == 1:
                    split(fq)
                act.wait_ge(job_done, n + JV)
                for t in range(NT):
                    f(v32[:, t, T:D], vb[1][t][:], ACT.Copy, scale=rms_col[:, t:t + 1]).then_inc(v_ready, 1)
                split(fq + 1)
                if L == 1:
                    act.wait_ge(fg_step, 3)
                    f(fg_soft, fg_soft, ACT.Exp).then_inc(fg_act, 1)
                    act.wait_ge(fg_act, 1)
                    f(fg_soft, fg_soft, ACT.Ln, bias=1.0).then_inc(fg_act, 1)
                    f(tmp_r[0], fg_one, ACT.Copy).then_inc(fg_act, 1)
                    act.wait_ge(fg_step, 7)
                    f(tmp_r[3], tmp_r[1].bitcast(F32), ACT.Copy, scale=-1.0).then_inc(fg_act, 1)
                    f(tmp_r[4], tmp_r[2].bitcast(F32), ACT.Copy, scale=-1.0).then_inc(fg_act, 1)
                split(fq + 2)
                act.wait_ge(v_ready, (2 * L + 2) * NT)
                if L == 0:
                    pair(0, "stick", 0, first=True)
                    loop(act, 1, STICK, lambda j: pair(0, "stick", j))
                    loop(act, STICK, NPAIR - 1, lambda j: pair(0, "dil", j))
                    pair(0, "dil", NPAIR - 1, last_pair=True)
                else:
                    pair(1, "fox", 0, first=True)
                    loop(act, 1, NPAIR - 1, lambda j: pair(1, "fox", j))
                    pair(1, "fox", NPAIR - 1, last_pair=True)
                for e in range(2):
                    heads_out((L + 1) * HEADS - 2 + e, e, blk(NPAIR - 1))

                def tail(stage, m, e):
                    act.wait_ge(x_new, m + ((stage - 1) * NB + 1))
                    alone()
                    gained(stage, m, e)
                    squares(stage, m, e)

                nj = out_job(L)

                def out_tiles(i):
                    for e in range(2):
                        split(nj + e + 1, i * 2, i)
                        tail(stage + 1, i * 2 + e, e)
                loop(act, 0, NB // 2, out_tiles)

                nj = ffn_job(L)

                def in_tile(i, first=False):
                    split(nj + 1, i * 2, i)
                    if first:
                        inverse_rms(stage + 1, False, 3 * L + 2)
                        nc.scalar.preload_act_table_set("sigmoid_and_others")
                    act.wait_ge(g_scaled, i + (L * NF + 1))
                    f(f_sig, f_gate, ACT.Sigmoid).then_inc(g_sig, 1)
                    split(nj + 2, i * 2, i)
                    act.wait_ge(act_ready, i + (L * NF + 1))
                    alone()
                    f(f_hi[:].rearrange("p (c t) -> p c t", c=NF)[:, blk(i), :], tmp[:], ACT.Copy).then_inc(f_hi_ready, 1)
                in_tile(0, first=True)
                loop(act, 1, NF, in_tile)

                nj = ffn_out_job(L)

                def ffn_tiles(i, last=False):
                    for e in range(2):
                        for c in range(NOUT):
                            k = NOUT * e + c + 1
                            if last and L == DEPTH - 1 and k == 2 * NOUT:
                                break
                            a, b = OUT_CHUNKS[k % NOUT]
                            split(nj + k, i * 6, i * 3, (b - a) * P)
                        tail(stage + 2, i * 2 + e, e)
                loop(act, 0, NB // 2 - 1, ffn_tiles)
                ffn_tiles(NB // 2 - 1, last=True)
            nc.scalar.preload_act_table_set("natural_log_exp_and_others")
            inverse_rms(2 * DEPTH, False, 3 * DEPTH)

        @block.vector
        def _(dve):
            v = nc.vector

            def split(n0, di=0, width=JOB, view=None):
                s = n0 % 2
                dve.wait_ge(w_hi_ready, di + (n0 + 1))
                view = view or (lambda w: w[:, s, 0:width])
                v.tensor_tensor(view(w_lo), view(w_raw), view(w_hi).bitcast(F32), ALU.subtract).then_inc(w_lo_ready, 1)

            def gained(stage, m):
                dve.wait_ge(h_hi_ready, m + (stage * NB + 1))
                v.scalar_tensor_tensor(h_lo[:, blk(m), :], x[:, blk(m), :], gains[:, stage, blk(m)],
                                       h_hi[:, blk(m), :].bitcast(F32), ALU.mult, ALU.subtract).then_inc(h_lo_ready, 1)

            def qk(L, kind, j, e):
                t = j * 2 + (L * HEADS + e)
                dve.wait_ge(job_done, j * 2 + (first_qk_job(L) + e + 1))
                if not (isinstance(t, int) and t == 0):
                    dve.wait_ge(qk_ready, t)
                sc, (hi, lo) = ((SCALE, (q_hi, q_lo)), (1.0, (k_hi, k_lo)))[e]
                if kind == "dil":
                    r = (j - STICK) * 4 + 2 * e
                    v.scalar_tensor_tensor(tmp[:], pb[e][:], sc, cosr[:], ALU.mult, ALU.mult)
                    v.stream_shuffle(tmp2[:], pb[e][:], SWAP).then_inc(rope_step, 1)
                    dve.wait_ge(rope_step, r + 1)
                    v.scalar_tensor_tensor(tmp2[:], tmp2[:], sc, sinr[:], ALU.mult, ALU.mult).then_inc(rope_step, 1)
                    dve.wait_ge(rope_step, r + 2)
                    v.tensor_tensor(tmp[:], tmp[:], tmp2[:], ALU.add).then_inc(qk_scaled, 1)
                else:
                    v.scalar_tensor_tensor(tmp[:], pb[e][:], sc, rms[:], ALU.mult, ALU.mult).then_inc(qk_scaled, 1)
                dve.wait_ge(qk_scaled, t + 1)
                v.tensor_copy(hi, tmp[:]).then_inc(qk_hi_ready, 1)
                dve.wait_ge(qk_hi_ready, t + 1)
                v.tensor_tensor(lo, tmp[:], hi.bitcast(F32), ALU.subtract).then_inc(qk_ready, 1)

            def heads_out(S, e, at):
                dve.wait_ge(o_hi_ready, S + 1)
                r = slice(DH * e, DH * (e + 1))
                v.tensor_tensor(o_lo[r, at, :], ob[e][r, :], o_hi[r, at, :].bitcast(F32), ALU.subtract).then_inc(o_lo_ready, 1)

            def pair(L, kind, j, next_kind, first=False, last_pair=False):
                for e in range(2):
                    S = j * 2 + (L * HEADS + e)
                    X = S - 2 * STICK
                    buf = s32[e]
                    for n, b in enumerate(range(NT) if kind != "stick" else reversed(range(NT))):
                        dve.wait_ge(z_ready, S * NT + (n + 1))
                        if kind == "stick":
                            v.tensor_scalar(buf[:, KO[b]:KO[b] + KW[b]], zb[b][:, 0:KW[b]], LINEAR, None,
                                            ALU.min).then_inc(min_ready, 1)
                        else:
                            v.tensor_reduce(nmax[:, b:b + 1], zb[b][:, 0:QW[b]], AX, ALU.max, negate=True).then_inc(max_ready, 1)
                    if e == 1 and not last_pair:
                        qk(L, next_kind, j + 1, 0)
                    if kind == "stick":
                        def high(n, b):
                            dve.wait_ge(sp_ready, S * NT + (n + 1))
                            c = slice(KO[b], KO[b] + KW[b])
                            v.tensor_copy(sp_hi[:, c], buf[:, c]).then_inc(sp_hi_ready, 1)
                        for n, b in enumerate(reversed(range(NT))):
                            dve.wait_ge(ln_ready, S * NT + (n + 1))
                            c = slice(KO[b], KO[b] + KW[b])
                            v.tensor_tensor(buf[:, c], zb[b][:, 0:KW[b]], buf[:, c], ALU.max).then_inc(sp_ready, 1)
                            if n:
                                high(n - 1, b + 1)
                        high(NT - 1, 0)
                    else:
                        for b in range(NT):
                            dve.wait_ge(rows_exp, X * NT + (b + 1))
                            c = slice(QO[b], QO[b] + QW[b])
                            if kind == "dil":
                                v.scalar_tensor_tensor(buf[:, c], buf[:, c], 1.0, mult[:, T - QW[b]:T], ALU.mult, ALU.mult,
                                                       accum_out=rsum[:, b:b + 1]).then_inc(rows_mult, 1)
                        if kind == "dil":
                            dve.wait_ge(rows_mult, X * NT + NT)
                        v.reciprocal(rinv[:], rsum[:]).then_inc(rows_inv, 1)
                        dve.wait_ge(rows_inv, X + 1)
                        for b in range(NT):
                            c = slice(QO[b], QO[b] + QW[b])
                            v.tensor_scalar(buf[:, c], buf[:, c], rinv[:, b:b + 1], None, ALU.mult).then_inc(rows_ready, 1)
                    if not last_pair:
                        split(first_qk_job(L) + 3 + e, j * 2)
                    if not first:
                        heads_out(S - 2, e, blk(j - 1))
                    if e == 1:
                        dve.wait_ge(vs_hi_ready, j + (L * NPAIR + 1))
                        v.tensor_tensor(v_lo[:], v32[:, :, bass.ds(j * P, P)], v_hi[:].bitcast(F32), ALU.subtract).then_inc(vs_ready, 1)
                        if not last_pair:
                            qk(L, next_kind, j + 1, 1)
                    for n, b in enumerate(range(NT) if kind != "stick" else reversed(range(NT))):
                        c = slice(KO[b], KO[b] + KW[b])
                        hi, lo = pt[e]
                        if kind == "stick":
                            dve.wait_ge(stick_exp, S * NT + (n + 1))
                            v.tensor_copy(hi[:, c], buf[:, c]).then_inc(pt_hi_ready, 1)
                        else:
                            dve.wait_ge(pt_hi_ready, S * NT + (n + 1))
                            v.tensor_tensor(lo[:, c], zb[b][:, 0:KW[b]], hi[:, c].bitcast(F32), ALU.subtract).then_inc(pt_lo_ready, 1)

            v.memset(eps[:], EPS).then_inc(eps_ready, 1)
            v.memset(ones[:], 1.0).then_inc(ones_ready, 1)
            dve.wait_ge(gains_loaded, 16)
            for m in range(NB):
                gained(0, m)
                if m < 2:
                    split(m)
            for L in range(DEPTH):
                stage = 2 * L
                n = JOB0[L]
                for c in range(JV):
                    if c == 4:
                        continue
                    if c > 0 or L > 0:
                        if c == JV - 1 and L == 1:
                            split(g_job, view=gate_cols)
                        else:
                            split(n + c + 1)
                    if c == 3:
                        split(n + 5)
                fq = first_qk_job(L)
                dve.wait_ge(rms_ready, stage + 1)
                if L == 0:
                    dve.wait_ge(const_loaded, 16 * 5)
                    v.tensor_tensor(cosr[:], cosr[:], rms[:], ALU.mult).then_inc(rope_ready, 1)
                    v.tensor_tensor(sinr[:], sinr[:], rms[:], ALU.mult).then_inc(rope_ready, 1)
                    dve.wait_ge(rope_ready, 2)
                    split(fq + 1)
                    qk(0, "stick", 0, 0)
                    split(fq + 2)
                    qk(0, "stick", 0, 1)
                    pair(0, "stick", 0, "stick", first=True)
                    loop(dve, 1, STICK - 1, lambda j: pair(0, "stick", j, "stick"))
                    pair(0, "stick", STICK - 1, "dil")
                    loop(dve, STICK, NPAIR - 1, lambda j: pair(0, "dil", j, "dil"))
                    pair(0, "dil", NPAIR - 1, None, last_pair=True)
                else:
                    split(fq)
                    split(fq + 1)
                    v.memset(fg_one, 1.0).then_inc(ones_ready, 1)
                    dve.wait_ge(job_done, g_job + 1)
                    v.tensor_tensor(fg_z, zb[0][0:HEADS, :], rms[0:HEADS, :], ALU.mult).then_inc(fg_step, 1)
                    dve.wait_ge(fg_step, 1)
                    v.tensor_scalar(fg_z, fg_z, bforget[:], None, ALU.add).then_inc(fg_step, 1)
                    dve.wait_ge(fg_step, 2)
                    v.tensor_scalar(fg_soft, fg_z, -1.0, LINEAR, ALU.mult, ALU.min).then_inc(fg_step, 1)
                    dve.wait_ge(fg_act, 2)
                    v.scalar_tensor_tensor(fg_z, fg_soft, -1.0, fg_z, ALU.mult, ALU.min).then_inc(fg_step, 1)
                    dve.wait_ge(fg_step, 4)
                    v.tensor_tensor_scan(fg_sum, fg_one, fg_z, 0.0, ALU.mult, ALU.add).then_inc(fg_step, 1)
                    dve.wait_ge(fg_step, 5)
                    v.tensor_copy(tmp_r[1], fg_sum).then_inc(fg_step, 1)
                    dve.wait_ge(fg_step, 6)
                    v.tensor_tensor(tmp_r[2], fg_sum, tmp_r[1].bitcast(F32), ALU.subtract).then_inc(fg_step, 1)
                    qk(1, "fox", 0, 0)
                    split(fq + 2)
                    qk(1, "fox", 0, 1)
                    pair(1, "fox", 0, "fox", first=True)
                    loop(dve, 1, NPAIR - 1, lambda j: pair(1, "fox", j, "fox"))
                    pair(1, "fox", NPAIR - 1, None, last_pair=True)
                for e in range(2):
                    heads_out((L + 1) * HEADS - 2 + e, e, blk(NPAIR - 1))

                def tail(stage, m, e, done, di):
                    dve.wait_ge(job_done, di + (done + 1))
                    v.tensor_tensor(x[:, blk(m), :], x[:, blk(m), :], pb[e][:], ALU.add).then_inc(x_new, 1)
                    if stage < 2 * DEPTH:
                        gained(stage, m)

                nj = out_job(L)

                def out_tiles(i):
                    for e in range(2):
                        split(nj + e + 1, i * 2)
                        tail(stage + 1, i * 2 + e, e, nj + e, i * 2)
                loop(dve, 0, NB // 2, out_tiles)

                nj = ffn_job(L)

                def in_tile(i, first=False):
                    t = i + L * NF
                    split(nj + 1, i * 2)
                    if first:
                        dve.wait_ge(rms_ready, stage + 2)
                    dve.wait_ge(job_done, i * 2 + (nj + 1))
                    v.tensor_tensor(f_gate, zb[0][:], rms[:], ALU.mult).then_inc(g_scaled, 1)
                    split(nj + 2, i * 2)
                    dve.wait_ge(g_sig, t + 1)
                    v.tensor_tensor(f_silu, f_gate, f_sig, ALU.mult).then_inc(g_silu, 1)
                    dve.wait_ge(job_done, i * 2 + (nj + 2))
                    v.tensor_tensor(f_up, zb[1][:], rms[:], ALU.mult).then_inc(u_scaled, 1)
                    dve.wait_ge(u_scaled, t + 1)
                    if not (first and L == 0):
                        dve.wait_ge(f_lo_ready, t)
                    v.tensor_tensor(tmp[:], f_silu, f_up, ALU.mult).then_inc(act_ready, 1)
                    dve.wait_ge(f_hi_ready, t + 1)
                    v.tensor_tensor(f_lo[:].rearrange("p (c t) -> p c t", c=NF)[:, blk(i), :], tmp[:],
                                    f_hi[:].rearrange("p (c t) -> p c t", c=NF)[:, blk(i), :].bitcast(F32),
                                    ALU.subtract).then_inc(f_lo_ready, 1)
                in_tile(0, first=True)
                loop(dve, 1, NF, in_tile)

                nj = ffn_out_job(L)

                def ffn_tiles(i, last=False):
                    for e in range(2):
                        for c in range(NOUT):
                            k = NOUT * e + c + 1
                            if last and L == DEPTH - 1 and k == 2 * NOUT:
                                break
                            a, b = OUT_CHUNKS[k % NOUT]
                            split(nj + k, i * 6, (b - a) * P)
                        tail(stage + 2, i * 2 + e, e, nj + NOUT * e + 2, i * 6)
                loop(dve, 0, NB // 2 - 1, ffn_tiles)
                ffn_tiles(NB // 2 - 1, last=True)
            dve.wait_ge(rms_ready, 2 * DEPTH + 1)
            for m in range(NB):
                v.tensor_tensor(y32[:, m, :], y32[:, m, :], rms[:], ALU.mult).then_inc(out_ready, 1)

        @block.gpsimd
        def _(pool):
            g = nc.gpsimd

            def squares(stage, m, e, first=False):
                pool.wait_ge(sq_ready, m + (stage * NB + 1))
                sq = (tmp, tmp2)[e][:]
                if first:
                    if stage:
                        pool.wait_ge(ssq_summed, stage)
                    g.tensor_copy(ssq[:], sq).then_inc(ssq_ready, 1)
                else:
                    pool.wait_ge(ssq_ready, m + stage * NB)
                    g.tensor_tensor(ssq[:], ssq[:], sq, ALU.add).then_inc(ssq_ready, 1)

            def stage_squares(stage):
                def two(i, first=False):
                    for e in range(2):
                        squares(stage, i * 2 + e, e, first and e == 0)
                two(0, first=True)
                loop(pool, 1, NB // 2, two)

            def stick_pair(j):
                for e in range(2):
                    S = j * 2 + e
                    for ready, hi, lo, done in ((sp_hi_ready, sp_hi, sp_lo, sp_lo_ready), (pt_hi_ready, *pt[e], pt_lo_ready)):
                        for n, b in enumerate(reversed(range(NT))):
                            pool.wait_ge(ready, S * NT + (n + 1))
                            c = slice(KO[b], KO[b] + KW[b])
                            g.tensor_tensor(lo[:, c], s32[e][:, c], hi[:, c].bitcast(F32), ALU.subtract).then_inc(done, 1)

            stage_squares(0)
            loop(pool, 0, STICK, stick_pair)
            for stage in range(1, 2 * DEPTH + 1):
                stage_squares(stage)


def _tables():
    q = np.arange(P)[:, None]
    k = np.arange(T)[None, :] - (T - P)
    dist = q - k
    mult = ((dist >= 0) & (dist <= 128)).astype(np.float32)
    mult += (dist >= 0) & (dist % 4 == 0)
    mult += (dist >= 0) & (dist % 16 == 0)
    dil = np.where(mult > 0, 0.0, MASKED)
    r = np.arange(P)
    causal = np.where(r[None, :] <= r[:, None], 0.0, MASKED)
    strict = np.where(r[:, None] < r[None, :], 0.0, MASKED)
    tri = np.where(r[:, None] >= r[None, :], -1.0, 0.0)
    masks = np.concatenate([dil, causal, strict, np.eye(P), tri], 1).astype(np.float32)
    half = ROT // 2
    inv = (np.float32(THETA) ** (-np.arange(half, dtype=np.float32) * np.float32(2.0) / np.float32(ROT))).astype(np.float32)
    ang = np.arange(T, dtype=np.float32)[None, :] * inv[:, None]
    cos, sin = np.cos(ang), np.sin(ang)
    rope = np.zeros((2, P, T), np.float32)
    rope[0] = 1.0
    for h in (0, DH):
        rope[0, h:h + half] = rope[0, h + half:h + ROT] = cos
        rope[1, h:h + half], rope[1, h + half:h + ROT] = -sin, sin
    return rope, mult.astype(np.float32), masks


def _tiles(w):
    k, n = w.shape
    return w.reshape(k // P, P, n // P, P).transpose(2, 1, 0, 3).reshape(n // P, P, k)


def _attention_jobs(w, w_o):
    q, k, v = w[:, 0:D], w[:, D:2 * D], w[:, 2 * D:3 * D]
    vj = v.reshape(4, 2, P, 2, T).transpose(3, 0, 2, 1, 4).reshape(JV, P, JOB)
    qk = np.stack([_tiles(q), _tiles(k)], 1).reshape(JQK, P, JOB)
    return np.ascontiguousarray(np.concatenate([vj, qk, _tiles(w_o)], 0))


def kernel(x, norm_mix, w_qkv_even, w_o_even, w_qkvf_odd, b_forget, w_o_odd, norm_ffn, w_ffn_in, w_ffn_out, norm_final):
    import concourse.bacc as _bacc
    from concourse.bass_utils import run_bass_kernel_spmd as _run

    a = np.asarray
    xt = a(x)[0].T.reshape(NB, P, T).transpose(1, 0, 2)
    gains = np.stack([a(norm_mix)[0], a(norm_ffn)[0], a(norm_mix)[1], a(norm_ffn)[1], a(norm_final)], 0)
    wf = a(w_qkvf_odd)[0][:, 3 * D:].reshape(NB, P, HEADS).transpose(1, 0, 2)
    win = np.stack([np.stack([_tiles(w[:, :DFF]), _tiles(w[:, DFF:])], 1).reshape(JIN, P, D) for w in a(w_ffn_in)])
    wout = np.stack([_tiles(w) for w in a(w_ffn_out)])
    rope, mult, masks = _tables()
    arrays = {
        "xt": xt, "gains": gains.reshape(2 * DEPTH + 1, NB, P).transpose(2, 0, 1),
        "wa0": _attention_jobs(a(w_qkv_even)[0], a(w_o_even)[0]),
        "wa1": _attention_jobs(a(w_qkvf_odd)[0], a(w_o_odd)[0]),
        "wf": wf, "win": win, "wout": wout, "bf": a(b_forget)[0][:, None],
        "rope": rope, "mult": mult, "masks": masks,
    }
    nc = _bacc.Bacc("TRN2", target_bir_lowering=False, num_devices=1)
    feed, args = {}, []
    for name, v in arrays.items():
        v = np.ascontiguousarray(v)
        feed[f"in_{name}"] = v
        args.append(nc.dram_tensor(f"in_{name}", v.shape, mybir.dt.from_np(v.dtype), kind="ExternalInput").ap())
    args.append(nc.dram_tensor("out_t", (P, NB, T), F32, kind="ExternalOutput").ap())
    trunk(nc, *args)
    r = _run(nc, [feed], core_ids=[0])
    out = r.results[0]["out_t"]
    return np.ascontiguousarray(out.transpose(2, 1, 0).reshape(T, D))[None]
```

```python
from contextlib import ExitStack

import numpy as np
import concourse.bass as bass
from concourse import mybir

F32 = mybir.dt.float32
F32R = mybir.dt.float32r
BF16 = mybir.dt.bfloat16
ALU = mybir.AluOpType
ACT = mybir.ActivationFunctionType
AX = mybir.AxisListType.X

P = 128
D, T, DH, DFF, DEPTH = 1024, 512, 64, 2816, 2
NB = D // P
NT = T // P
NF = DFF // P
NPAIR = D // (2 * DH)
HEADS = 2 * NPAIR
STICK = NPAIR // 2
SCALE = DH ** -0.5
EPS = 1e-5
THETA = 500000.0
ROT = DH // 4
CONSTS = 7
MASKED = -1e30
JOB = 8 * P

KW = [T - b * P for b in range(NT)]
KO = [sum(KW[:b]) for b in range(NT)]
QW = [(b + 1) * P for b in range(NT)]
QO = [sum(QW[:b]) for b in range(NT)]
TRI = sum(KW)
PACK = {4 * P: (0, 0), 3 * P: (1, 0), P: (1, 3 * P), 2 * P: (2, 0)}
KR, QR = (2, 3, 1, 0), (1, 0, 2, 3)
DONE, PASSED = (2, 3, 3, 4), (1, 3, 3, 4)

JV, JQK, JO, JIN, NOUT = 8, 2 * NPAIR, NB, 2 * NF, 3
OUT_CHUNKS = [(0, 8), (8, 15), (15, 22)]
JATT = [JV + JQK + JO, JV + 1 + JQK + JO]
FILL = [(range(0, 3),), (range(3, 5), range(5, 6))]
JOB0 = [0, JATT[0] + JIN + NOUT * NB]
SWAP = [(i + ROT // 2) % ROT if i < ROT else i for i in range(32)]


def loop(eng, start, end, body):
    if end - start == 1:
        body(start)
    elif end > start:
        with eng.Fori(start, end) as i:
            body(i)


def blk(i):
    return bass.ds(i, 1)


def trunk(nc, xt_d, gains_d, wa0_d, wa1_d, wf_d, win_d, wout_d, bf_d, rope_d, mult_d, masks_d, out_d):
    ctx = ExitStack()
    with ctx:
        def sb(name, shape, dt=F32):
            return ctx.enter_context(nc.sbuf_tensor(name, shape, dt))

        def bank(name):
            return ctx.enter_context(nc.psum_tensor(name, [P, T], F32))

        def sem(name):
            return ctx.enter_context(nc.semaphore(name))

        x = sb("x", [P, NB, T])
        h_hi = sb("h_hi", [P, NB, T], F32R)
        h_lo = sb("h_lo", [P, NB, T], F32R)
        w_raw = sb("w_raw", [P, 2, JOB])
        w_hi = sb("w_hi", [P, 2, JOB], F32R)
        w_lo = sb("w_lo", [P, 2, JOB], F32R)
        f_hi = sb("f_hi", [P, NF * T], F32R)
        f_lo = sb("f_lo", [P, NF * T], F32R)

        used = [0]

        def parts(n, *shape):
            a, used[0] = used[0], used[0] + n
            assert used[0] <= NF * T
            return f_hi[:, a:a + n], f_lo[:, a:a + n]

        o_hi, o_lo = (v.rearrange("p (c t) -> p c t", c=NB) for v in parts(NB * T))
        pt = [parts(TRI) for _ in range(2)]
        sp_hi, sp_lo = parts(TRI)
        st, mv, mv2, st2 = (parts(T) for _ in range(4))
        v_hi, v_lo = (v.rearrange("p (c t) -> p c t", c=NT) for v in parts(NT * P))
        neg_tri, neg_one = parts(P)

        v32 = sb("v32", [P, NT, D])
        s32 = [sb(f"s32_{i}", [P, TRI]) for i in range(2)]
        tmp = sb("tmp", [P, T])
        tmp2 = sb("tmp2", [P, T])
        tmp3 = sb("tmp3", [P, T])
        col_tmp = sb("col_tmp", [P, NT])
        rms = sb("rms", [P, T])
        rms_col = sb("rms_col", [P, NT])
        cosr = sb("cosr", [P, T])
        sinr = sb("sinr", [P, T])
        mult = sb("mult", [P, T])
        ssq = sb("ssq", [P, T])
        ones = sb("ones", [P, P])
        ident = sb("ident", [P, P])
        ident_b = sb("ident_b", [P, P], BF16)
        m_dil = sb("m_dil", [P, T], BF16)
        m_causal = sb("m_causal", [P, P], BF16)
        m_strict = sb("m_strict", [P, P], BF16)
        gains = sb("gains", [P, 2 * DEPTH + 1, NB])
        bforget = sb("bforget", [HEADS, 1])
        eps = sb("eps", [P, 1])
        nmax = sb("nmax", [P, NT])
        rsum = sb("rsum", [P, NT])
        rinv = sb("rinv", [P, NT])
        f_rows = nc.dram_tensor("f_rows", (2, 4, HEADS, T), F32).ap()
        masks32 = v32[:, 0, :]

        zb = [[bank(f"zb{e}{b}") for b in range(3)] for e in range(2)]
        pb = bank("pb")
        ob = bank("ob")
        sums, col_sums = ob, zb[1][2]
        gate, up = zb[1][0], zb[1][1]
        outs = [pb, zb[0][0]]
        vb = [[*zb[0], zb[1][0]], [zb[1][1], pb, sums, col_sums]]
        logits = vb[1][0]

        def zt(e, w):
            b, at = PACK[w]
            return zb[e][b][:, at:at + w]

        x_loaded = [sem(f"x_loaded{i}") for i in range(4)]
        gains_loaded, const_loaded, const_ready, ones_ready = (sem(n) for n in ("gains_loaded", "const_loaded", "const_ready", "ones_ready"))
        w_loaded = [sem("w_loaded0"), sem("w_loaded1")]
        w_hi_ready, w_lo_ready, job_done = sem("w_hi_ready"), sem("w_lo_ready"), sem("job_done")
        h_hi_ready, h_lo_ready, x_new = sem("h_hi_ready"), sem("h_lo_ready"), sem("x_new")
        sq_ready, ssq_ready, ssq_summed, ln_done, rms_ready = (sem(n) for n in ("sq_ready", "ssq_ready", "ssq_summed", "ln_done", "rms_ready"))
        v_ready = sem("v_ready")
        qk_scaled, qk_hi_ready, qk_lo_ready, qk_dup_ready = (sem(n) for n in ("qk_scaled", "qk_hi_ready", "qk_lo_ready", "qk_dup_ready"))
        vs_hi_ready, vs_ready = sem("vs_hi_ready"), sem("vs_ready")
        z_ready, abs_ready, exp_done, ln_ready = (sem(n) for n in ("z_ready", "abs_ready", "exp_done", "ln_ready"))
        sp_ready, sp_hi_ready, sp_lo_ready = sem("sp_ready"), sem("sp_hi_ready"), sem("sp_lo_ready")
        max_ready, rows_exp, rows_mult, rows_inv, rows_ready = (sem(n) for n in ("max_ready", "rows_exp", "rows_mult", "rows_inv", "rows_ready"))
        a_hi_ready, a_lo_ready = sem("a_hi_ready"), sem("a_lo_ready")
        second_ready, stick_exp, pt_hi_ready, pt_lo_ready = (sem(n) for n in ("second_ready", "stick_exp", "pt_hi_ready", "pt_lo_ready"))
        o_summed, o_hi_ready, o_lo_ready = sem("o_summed"), sem("o_hi_ready"), sem("o_lo_ready")
        g_scaled, g_sig, g_silu, u_scaled, act_ready, f_hi_ready, f_lo_ready = (sem(n) for n in (
            "g_scaled", "g_sig", "g_silu", "u_scaled", "act_ready", "f_hi_ready", "f_lo_ready"))
        fg_step, fg_act, rows_stored, rows_loaded = (sem(n) for n in ("fg_step", "fg_act", "rows_stored", "rows_loaded"))
        eps_ready, col_ready, rms_raw, newton = sem("eps_ready"), sem("col_ready"), sem("rms_raw"), sem("newton")
        rows_clear = sem("rows_clear")
        rope_shuffled, rope_sin, mv2_clear = sem("rope_shuffled"), sem("rope_sin"), sem("mv2_clear")
        rope_ready, out_ready, out_stored = sem("rope_ready"), sem("out_ready"), sem("out_stored")

        f_gate, f_sig, f_silu, f_up = s32[0][:, 0:T], s32[0][:, T:2 * T], s32[1][:, 0:T], s32[1][:, T:2 * T]
        fg_z, fg_soft, fg_sum, fg_one = (v[0:HEADS, :] for v in (f_gate, f_sig, f_silu, f_up))
        sin_q = ssq[:]
        y32 = v32[:].rearrange("p a b -> p (a b)").rearrange("p (m t) -> p m t", m=NB)
        g_job = JOB0[1]

        def gate_cols(w):
            return w[:, g_job % 2, :].rearrange("p (c n) -> p c n", c=NB)[:, :, 0:HEADS]

        tmp_r = [v[0:HEADS, :] for v in (sp_hi[:, 0:T], sp_hi[:, T:2 * T], sp_lo[:, 0:T], sp_lo[:, T:2 * T], pt[1][0][:, 0:T])]

        block = ctx.enter_context(nc.Block())

        def first_qk_job(L):
            return JOB0[L] + JV + L

        def out_job(L):
            return JOB0[L] + JATT[L] - JO

        def ffn_job(L):
            return JOB0[L] + JATT[L]

        def ffn_out_job(L):
            return ffn_job(L) + JIN

        def own(e):
            return slice(DH * e, DH * (e + 1))

        def other(e):
            return own(1 - e)

        def is_st(kind, i):
            return (i % 2 == 1) == (kind == "stick")

        def pieces(eng, f_hi_part, f_lo_part, f_dup, L, kind, jn, which):
            def tiles(i):
                e = i // 2
                return e, (tmp, tmp2)[i % 2], (st if is_st(kind, i) else mv)[e]
            if f_hi_part:
                for i in which:
                    e, t, to = tiles(i)
                    eng.wait_ge(qk_scaled, jn * 2 + (L * HEADS + 1 + i % 2))
                    if not isinstance(jn, int) or jn > 0:
                        eng.wait_ge(z_ready, jn * (2 * NT) + (L * HEADS + e - 1) * NT)
                    f_hi_part(to[own(e), :], t[own(e), :]).then_inc(qk_hi_ready, 1)
            if f_lo_part:
                for i in which:
                    e, t, hi = tiles(i)
                    eng.wait_ge(qk_hi_ready, jn * 4 + (4 * L * NPAIR + i + 1))
                    out = st[e][other(e), :] if is_st(kind, i) else mv2[e][own(e), :]
                    f_lo_part(out, t[own(e), :], hi[own(e), :].bitcast(F32)).then_inc(qk_lo_ready, 1)
            if f_dup:
                for i in which:
                    e, t, hi = tiles(i)
                    if not is_st(kind, i) or kind == "fox":
                        eng.wait_ge(qk_hi_ready, jn * 4 + (4 * L * NPAIR + i + 1))
                        out = st2[e][own(e), :] if is_st(kind, i) else mv[e][other(e), :]
                        f_dup(out, hi[own(e), :].bitcast(F32)).then_inc(qk_dup_ready, 1)

        @block.sync
        def _(sp):
            def load(n0, di, half, src, width=JOB):
                s = n0 % 2
                if n0 >= 2:
                    sp.wait_ge(w_hi_ready, di + (n0 - 1))
                    sp.wait_ge(w_lo_ready, di + (n0 - 1))
                sp.dma_start(w_raw[:, s, 0:width], src).then_inc(w_loaded[s], 16)

            def loads(n0, count, dram, first):
                def two(i):
                    for e in range(2):
                        load(n0 + e, i * 2, i, dram[blk(i * 2 + (first + e))].rearrange("o p n -> p (o n)"))
                loop(sp, 0, count // 2, two)

            sp.dma_start(gains[:], gains_d).then_inc(gains_loaded, 16)
            for i in range(4):
                sp.dma_start(x[:, 2 * i:2 * i + 2, :], xt_d[:, 2 * i:2 * i + 2, :]).then_inc(x_loaded[i], 16)
                if i < 2:
                    load(i, 0, 0, wa0_d[i])
            sp.dma_start(masks32, masks_d).then_inc(const_loaded, 16)
            sp.dma_start(cosr[:], rope_d[0]).then_inc(const_loaded, 16)
            sp.dma_start(sinr[:], rope_d[1]).then_inc(const_loaded, 16)
            sp.dma_start(mult[:], mult_d).then_inc(const_loaded, 16)
            sp.dma_start(bforget[:], bf_d).then_inc(const_loaded, 16)

            def f_load(j):
                for e in range(2):
                    for ab, rows in enumerate((st2[e], mv2[e])):
                        sp.dma_start(rows[DH * (1 - e):DH * (1 - e) + 4, :].bitcast(F32),
                                     f_rows[ab][:, blk(j * 2 + e), :].rearrange("r o t -> r (o t)")).then_inc(rows_loaded, 16)

            for L in range(DEPTH):
                n = JOB0[L]
                wa = (wa0_d, wa1_d)[L]
                if L == 0:
                    loads(2, JATT[0] - 2, wa, 2)
                else:
                    sp.wait_ge(w_hi_ready, g_job - 1)
                    sp.wait_ge(w_lo_ready, g_job - 1)
                    sp.dma_start(gate_cols(w_raw), wf_d).then_inc(w_loaded[g_job % 2], 16)
                    loads(n + 1, JV - 2, wa, 0)
                    sp.wait_ge(fg_step, 7)
                    sp.wait_ge(fg_act, 5)
                    one, hi, lo, nhi, nlo = (tmp_r[i] for i in range(5))
                    for ab, rows in enumerate(((one, one, hi, lo), (nhi, nlo, one, one))):
                        for r, src in enumerate(rows):
                            sp.dma_start(f_rows[ab, r], src.bitcast(F32)).then_inc(rows_stored, 16)
                    loads(n + 1 + JV - 2, 2, wa, JV - 2)
                    sp.wait_ge(rows_stored, 16 * 8)
                    sp.wait_ge(rows_clear, 4)
                    f_load(0)
                    for r in range(JV, JV + 5):
                        load(n + 1 + r, 0, 0, wa[r])

                    def pair(j):
                        for e in range(2):
                            r = JV + 5 + e
                            load(n + 1 + r, j * 2, j, wa[blk(j * 2 + r)].rearrange("o p n -> p (o n)"))
                        sp.wait_ge(z_ready, j * (2 * NT) + (HEADS + 2) * NT)
                        f_load(j + 1)
                    loop(sp, 0, NPAIR - 1, pair)
                    done = JV + 5 + 2 * (NPAIR - 1)
                    load(n + 1 + done, 0, 0, wa[done])
                    loads(n + 2 + done, JV + JQK + JO - done - 1, wa, done + 1)
                loads(ffn_job(L), JIN, win_d[L], 0)
                no = ffn_out_job(L)

                def two_tiles(i):
                    for e in range(2):
                        for c, (a, b) in enumerate(OUT_CHUNKS):
                            k = NOUT * e + c
                            load(no + k, i * 6, i * 3,
                                 wout_d[L][blk(i * 2 + e), :, a * P:b * P].rearrange("o p n -> p (o n)"), (b - a) * P)
                loop(sp, 0, NB // 2, two_tiles)

            for m in range(NB):
                sp.wait_ge(out_ready, m + 1)
                sp.dma_start(out_d[:, m, :], v32[:].rearrange("p a b -> p (a b)")[:, m * T:(m + 1) * T]).then_inc(out_stored, 16)
            sp.wait_ge(out_stored, 16 * NB)


        @block.tensor
        def _(pe):
            mm = nc.tensor.matmul

            def job_ready(n0, di):
                pe.wait_ge(w_hi_ready, di + (n0 + 1))
                pe.wait_ge(w_lo_ready, di + (n0 + 1))

            def product(out, s, chunks, hi, lo, start=True, stop=True, wait=None, at=0, ends=True):
                for c, k in enumerate(chunks, at):
                    if wait:
                        wait(k)
                    wh, wl = w_hi[:, s, c * P:(c + 1) * P], w_lo[:, s, c * P:(c + 1) * P]
                    mm(out, wh, hi[:, k, :], start=start and c == 0, stop=False)
                    mm(out, wh, lo[:, k, :], start=False, stop=False)
                    last = mm(out, wl, hi[:, k, :], start=False, stop=stop and c == at + len(chunks) - 1)
                if ends:
                    last.then_inc(job_done, 1)

            def h_ready(stage):
                def wait(k):
                    pe.wait_ge(h_hi_ready, stage * NB + k + 1)
                    pe.wait_ge(h_lo_ready, stage * NB + k + 1)
                return wait

            def sum_squares(stage, cols):
                pe.wait_ge(ssq_ready, (stage + 1) * NB)
                last = mm(sums[:], ones[:], ssq[:], start=True, stop=True)
                if cols:
                    for t in range(NT):
                        last = mm(col_sums[:, t:t + 1], ssq[:, t * P:(t + 1) * P], ones[:, 0:1], start=True, stop=True)
                last.then_inc(ssq_summed, 1)

            def read(kind, S):
                if kind == "stick":
                    pe.wait_ge(stick_exp, S * NT + NT)
                else:
                    pe.wait_ge(pt_hi_ready, (S - 2 * STICK) * NT + NT)
                    pe.wait_ge(pt_lo_ready, (S - 2 * STICK) * NT + NT)

            def scores(kind, S, e):
                order = list(range(NT) if kind != "stick" else reversed(range(NT)))
                for b in order:
                    at, w, move = ((slice(b * P, (b + 1) * P), KW[b], slice(b * P, T)) if kind == "stick" else
                                   (slice(b * P, (b + 1) * P), QW[b], slice(0, QW[b])))
                    out = zt(e, w)
                    mm(out, st[e][:, at], mv[e][:, move], start=w != 3 * P, stop=False, skip_group_check=True)
                    mm(out, (st2 if kind == "fox" else st)[e][:, at], mv2[e][:, move], start=False, stop=False,
                       skip_group_check=True)
                for b in order:
                    w = KW[b] if kind == "stick" else QW[b]
                    mask, at = ((m_strict[:], slice(0, P)) if kind == "stick" else
                                (m_dil[:, T - w:T], slice(0, w)) if kind == "dil" else (m_causal[:], slice(w - P, w)))
                    mm(zt(e, w)[:, at], ident_b[:], mask, start=False, stop=True, skip_group_check=True).then_inc(z_ready, 1)

            def suffix_sums(S, e):
                pe.wait_ge(sp_hi_ready, S * NT + NT)
                pe.wait_ge(sp_lo_ready, S * NT + NT)
                for b in reversed(range(NT)):
                    out = zt(e, KW[b])
                    for later in range(b + 1, NT):
                        for v in (sp_hi, sp_lo):
                            mm(out[:, (later - b) * P:KW[b]], neg_one, v[:, KO[later]:KO[later] + KW[later]],
                               start=False, stop=False, skip_group_check=True)
                    for v in (sp_hi, sp_lo):
                        last = mm(out, neg_tri, v[:, KO[b]:KO[b] + KW[b]],
                                  start=False, stop=v is sp_lo, skip_group_check=True)
                    last.then_inc(second_ready, 1)

            def transposes(S, e):
                pe.wait_ge(rows_ready, (S - 2 * STICK) * NT + NT)
                for b in range(NT):
                    for k in reversed(range(b + 1)):
                        last = nc.tensor.transpose(zt(e, KW[k])[:, (b - k) * P:(b - k + 1) * P],
                                                   s32[e][:, QO[b] + k * P:QO[b] + (k + 1) * P], ident[:])
                        if b == NT - 1:
                            last.then_inc(second_ready, 1)

            def second(kind, S, e):
                (suffix_sums if kind == "stick" else transposes)(S, e)

            def values(S, kind, e):
                if kind == "stick":
                    pe.wait_ge(a_hi_ready, S * NT + NT)
                    pe.wait_ge(a_lo_ready, S * NT + NT)
                else:
                    pe.wait_ge(pt_hi_ready, (S - 2 * STICK) * NT + NT)
                    pe.wait_ge(pt_lo_ready, (S - 2 * STICK) * NT + NT)
                hi, lo = pt[e]
                for b in range(NT):
                    out, c = ob[:, b * P:T], slice(KO[b], KO[b] + KW[b])
                    mm(out, v_hi[:, b, :], hi[:, c], start=b == 0, stop=False)
                    mm(out, v_hi[:, b, :], lo[:, c], start=False, stop=False)
                    last = mm(out, v_lo[:, b, :], hi[:, c], start=False, stop=b == NT - 1)
                last.then_inc(o_summed, 1)

            def out_part(L, n, blocks):
                def wait(k):
                    pe.wait_ge(o_hi_ready, L * HEADS + 2 * k + 2)
                    pe.wait_ge(o_lo_ready, L * HEADS + 2 * k + 2)
                job = out_job(L) + n
                job_ready(job, 0)
                product(outs[n][:], job % 2, blocks, o_hi, o_lo, stop=blocks[-1] == NB - 1, wait=wait,
                        at=blocks[0], ends=blocks[-1] == NB - 1)

            def pair(L, kind, j, before=None, projects=2, first=False, fill=(), ropes=False):
                for e in range(2):
                    S = j * 2 + (L * HEADS + e)
                    pe.wait_ge(qk_lo_ready, j * 4 + (4 * L * NPAIR + 2 * e + 2))
                    pe.wait_ge(qk_dup_ready, j * 4 + (2 * NPAIR + 2 * e + 2) if kind == "fox" else j * 2 + (e + 1))
                    if e == 0 and kind == "fox":
                        pe.wait_ge(rows_loaded, j * 64 + 64)
                    if not first:
                        read(before, S - 2)
                    scores(kind, S, e)
                    if not (first and e == 0):
                        second(before if e == 0 else kind, S - 1, 1 - e)
                    if e < projects:
                        n0 = first_qk_job(L) + 3 + e
                        job_ready(n0, j * 2)
                        if ropes:
                            pe.wait_ge(rope_shuffled, j * 2 + (3 + e - 2 * STICK))
                        else:
                            pe.wait_ge(qk_scaled, j * 2 + (L * HEADS + 3 + e))
                        product(pb[:], n0 % 2, range(NB), h_hi, h_lo)
                    elif fill:
                        if fill[0][0] == 0:
                            pe.wait_ge(qk_scaled, (L + 1) * HEADS)
                        out_part(L, 0, fill[e - projects])
                    if not (first and e == 0):
                        if not first:
                            pe.wait_ge(o_hi_ready, S - 1)
                            pe.wait_ge(o_lo_ready, S - 1)
                        if e == 1:
                            pe.wait_ge(vs_ready, j + (L * NPAIR + 1))
                        values(S - 1, before if e == 0 else kind, 1 - e)

            pe.wait_ge(ones_ready, 1)
            for L in range(DEPTH):
                stage = 2 * L
                n = JOB0[L] + L
                if L == 1:
                    job_ready(g_job, 0)
                    product(logits[:], g_job % 2, range(NB), h_hi, h_lo, wait=h_ready(stage))
                    sum_squares(stage, True)
                for half in range(2):
                    for c2 in range(4):
                        job = n + 4 * half + c2
                        job_ready(job, 0)
                        s = job % 2
                        for c in range(2):
                            k = 2 * c2 + c
                            if half == 0:
                                h_ready(stage)(k)
                            wh, wl = w_hi[:, s, c * T:(c + 1) * T], w_lo[:, s, c * T:(c + 1) * T]
                            for t in range(NT):
                                out, tt = vb[half][t][:], slice(t * P, (t + 1) * P)
                                if half == 1 and k == 0 and t == 0 and L == 1:
                                    pe.wait_ge(fg_step, 1)
                                if half == 1 and k == 0 and t == 2:
                                    pe.wait_ge(rms_ready, stage + 1)
                                mm(out, h_hi[:, k, tt], wh, start=k == 0, stop=False)
                                mm(out, h_hi[:, k, tt], wl, start=False, stop=False)
                                last = mm(out, h_lo[:, k, tt], wh, start=False, stop=k == NB - 1)
                        last.then_inc(job_done, 1)
                    if half == 0 and L == 0:
                        sum_squares(stage, True)
                pe.wait_ge(v_ready, (2 * L + 2) * NT)
                for t in range(3):
                    n0 = first_qk_job(L) + t
                    job_ready(n0, 0)
                    if t == 2:
                        pe.wait_ge(qk_scaled, L * HEADS + 1)
                    product((pb, ob, pb)[t][:], n0 % 2, range(NB), h_hi, h_lo)
                if L == 0:
                    pe.wait_ge(const_ready, CONSTS)
                    pe.wait_ge(mv2_clear, 1)
                    pair(0, "stick", 0, first=True)
                    loop(pe, 1, STICK - 1, lambda j: pair(0, "stick", j, "stick"))
                    pair(0, "stick", STICK - 1, "stick", ropes=True)
                    pair(0, "dil", STICK, "stick", ropes=True)
                    loop(pe, STICK + 1, NPAIR - 2, lambda j: pair(0, "dil", j, "dil", ropes=True))
                    pair(0, "dil", NPAIR - 2, "dil", projects=1, fill=FILL[0], ropes=True)
                    pair(0, "dil", NPAIR - 1, "dil", projects=0, fill=FILL[1])
                else:
                    pair(1, "fox", 0, first=True)
                    loop(pe, 1, NPAIR - 2, lambda j: pair(1, "fox", j, "fox"))
                    pair(1, "fox", NPAIR - 2, "fox", projects=1, fill=FILL[0])
                    pair(1, "fox", NPAIR - 1, "fox", projects=0, fill=FILL[1])
                S = (L + 1) * HEADS
                second("fox", S - 1, 1)
                out_part(L, 0, range(6, 7))
                read("fox", S - 2)
                out_part(L, 1, range(7))
                pe.wait_ge(o_hi_ready, S - 1)
                pe.wait_ge(o_lo_ready, S - 1)
                values(S - 1, "fox", 1)
                for n in range(2):
                    out_part(L, n, range(7, 8))

                def added(stage, i, e):
                    pe.wait_ge(x_new, i * 2 + ((stage - 1) * NB + e - 1))

                nj = out_job(L)

                def out_tiles(i):
                    for e in range(2):
                        added(stage + 1, i, e)
                        job_ready(nj + e, i * 2)
                        product(outs[e][:], (nj + e) % 2, range(NB), o_hi, o_lo)
                loop(pe, 1, NB // 2, out_tiles)

                nj = ffn_job(L)

                def in_tile(i, first=False):
                    if not first:
                        pe.wait_ge(g_scaled, i + L * NF)
                    job_ready(nj, i * 2)
                    product(gate[:], nj % 2, range(NB), h_hi, h_lo, wait=h_ready(stage + 1) if first else None)
                    if first:
                        sum_squares(stage + 1, False)
                    else:
                        pe.wait_ge(u_scaled, i + L * NF)
                    job_ready(nj + 1, i * 2)
                    product(up[:], (nj + 1) % 2, range(NB), h_hi, h_lo)
                in_tile(0, first=True)
                loop(pe, 1, NF, in_tile)

                nj = ffn_out_job(L)
                fh = f_hi[:].rearrange("p (c t) -> p c t", c=NF)
                fl = f_lo[:].rearrange("p (c t) -> p c t", c=NF)

                def f_ready(k):
                    pe.wait_ge(f_hi_ready, L * NF + k + 1)
                    pe.wait_ge(f_lo_ready, L * NF + k + 1)

                def ffn_tiles(i, first=False):
                    for e in range(2):
                        if not first:
                            added(stage + 2, i, e)
                        for c, (a, b) in enumerate(OUT_CHUNKS):
                            k = NOUT * e + c
                            job_ready(nj + k, i * 6)
                            product(outs[e][:], (nj + k) % 2, range(a, b), fh, fl, c == 0, c == NOUT - 1,
                                    f_ready if first and e == 0 else None)
                ffn_tiles(0, first=True)
                loop(pe, 1, NB // 2, ffn_tiles)
            sum_squares(2 * DEPTH, False)

        @block.scalar
        def _(act):
            f = nc.scalar.activation

            def alone():
                nc.scalar.nop(nofuse=True)

            def split(n0, di=0, half=0, width=JOB, view=None):
                s = n0 % 2
                act.wait_ge(w_loaded[s], half * 16 + 16 * (n0 // 2 + 1))
                if n0 >= 2:
                    act.wait_ge(job_done, di + (n0 - 1))
                view = view or (lambda w: w[:, s, 0:width])
                f(view(w_hi), view(w_raw), ACT.Copy).then_inc(w_hi_ready, 1)

            def squares(stage, m, e, first=False):
                if not first:
                    act.wait_ge(ssq_ready, m + (stage * NB - 1))
                    alone()
                f((tmp, tmp2)[e][:], x[:, m if isinstance(m, slice) else blk(m), :], ACT.Square).then_inc(sq_ready, 1)

            def gained(stage, m, e):
                g = gains[:, stage, blk(m)]
                if stage < 2 * DEPTH:
                    f(h_hi[:, blk(m), :], x[:, blk(m), :], ACT.Copy, scale=g).then_inc(h_hi_ready, 1)
                else:
                    f(y32[:, blk(m), :], x[:, blk(m), :], ACT.Copy, scale=g).then_inc(h_hi_ready, 1)

            def inverse_rms(stage, cols, lns):
                act.wait_ge(ssq_summed, stage + 1)
                f(rms[:], sums[:], ACT.Ln, bias=eps[:], scale=1.0 / D).then_inc(ln_done, 1)
                if cols:
                    f(rms_col[:], col_sums[:, 0:NT], ACT.Ln, bias=eps[:], scale=1.0 / D).then_inc(ln_done, 1)
                    act.wait_ge(ln_done, lns + 2)
                    f(rms_col[:], rms_col[:], ACT.Exp, scale=-0.5)
                act.wait_ge(ln_done, lns + 1)
                f(rms[:], rms[:], ACT.Exp, scale=-0.5).then_inc(rms_raw, 1)

            def heads_out(S, e, at):
                act.wait_ge(o_summed, S + 1)
                alone()
                r = slice(DH * e, DH * (e + 1))
                f(o_hi[r, at, :], ob[r, :], ACT.Copy).then_inc(o_hi_ready, 1)

            def finish(kind, S, e):
                for n, b in enumerate(KR):
                    act.wait_ge(second_ready, S * NT + DONE[n])
                    c = slice(KO[b], KO[b] + KW[b])
                    if kind == "stick":
                        f(s32[e][:, c], zt(e, KW[b]), ACT.Exp).then_inc(stick_exp, 1)
                    else:
                        f(pt[e][0][:, c], zt(e, KW[b]), ACT.Copy).then_inc(pt_hi_ready, 1)

            def hi_part(to, x):
                return f(to, x, ACT.Copy)

            def pair(L, kind, j, before=None, splits=True):
                for e in range(2):
                    S = j * 2 + (L * HEADS + e)
                    buf = s32[e]
                    if before:
                        heads_out(S - 2, e, blk(j - 1))
                    if e == 1:
                        f(v_hi[:], v32[:, :, bass.ds(j * P, P)], ACT.Copy).then_inc(vs_hi_ready, 1)
                    if kind == "stick":
                        for n, b in enumerate(KR):
                            act.wait_ge(z_ready, S * NT + DONE[n])
                            f(buf[:, KO[b]:KO[b] + KW[b]], zt(e, KW[b]), ACT.Abs).then_inc(abs_ready, 1)
                    else:
                        X = S - 2 * STICK
                        for n, b in enumerate(QR):
                            act.wait_ge(max_ready, X * NT + PASSED[n])
                            sums = {"accum_out": rsum[:, b:b + 1]} if kind == "fox" else {}
                            f(buf[:, QO[b]:QO[b] + QW[b]], zt(e, QW[b]), ACT.Exp,
                              bias=nmax[:, b:b + 1], **sums).then_inc(rows_exp, 1)
                    if before or e == 1:
                        finish(before if e == 0 else kind, S - 1, 1 - e)
                    if splits and kind != "stick":
                        pieces(act, hi_part, None, None, L, kind, j + 1, range(1, 4) if e else range(1))
                    if splits:
                        split(first_qk_job(L) + 4 + e, j * 2, j)
                    if kind == "dil":
                        act.wait_ge(rows_inv, X + 1)
                        for b in range(NT):
                            c = slice(QO[b], QO[b] + QW[b])
                            f(buf[:, c], buf[:, c], ACT.Copy, scale=rinv[:, b:b + 1]).then_inc(rows_ready, 1)
                    if kind == "stick":
                        for n, b in enumerate(KR):
                            act.wait_ge(abs_ready, S * NT + (n + 1))
                            c = slice(KO[b], KO[b] + KW[b])
                            f(buf[:, c], buf[:, c], ACT.Exp, scale=-1.0).then_inc(exp_done, 1)
                        for n, b in enumerate(KR):
                            act.wait_ge(exp_done, S * NT + (n + 1))
                            c = slice(KO[b], KO[b] + KW[b])
                            f(buf[:, c], buf[:, c], ACT.Ln, bias=1.0).then_inc(ln_ready, 1)

            nc.scalar.preload_act_table_set("natural_log_exp_and_others")
            act.wait_ge(gains_loaded, 16)
            act.wait_ge(eps_ready, 1)
            for m in range(NB):
                act.wait_ge(x_loaded[m // 2], 16)
                gained(0, m, m % 2)
                squares(0, m, m % 2, first=m < 2)
                if m < 2:
                    split(m)
            act.wait_ge(const_loaded, 16 * 5)
            act.wait_ge(ones_ready, 1)
            for dst, a, b in ((m_dil[:], 0, T), (m_causal[:], T, T + P), (m_strict[:], T + P, T + 2 * P),
                              (ident_b[:], T + 2 * P, T + 3 * P), (ident[:], T + 2 * P, T + 3 * P), (neg_tri, T + 3 * P, D)):
                f(dst, masks32[:, a:b], ACT.Copy).then_inc(const_ready, 1)
            f(neg_one, ones[:], ACT.Copy, scale=-1.0).then_inc(const_ready, 1)

            for L in range(DEPTH):
                stage = 2 * L
                n = JOB0[L] + L
                fq = first_qk_job(L)
                if L == 1:
                    nc.scalar.preload_act_table_set("natural_log_exp_and_others")
                    split(n)
                    inverse_rms(stage, True, 3 * L)
                    split(n + 1)
                    act.wait_ge(fg_step, 3)
                    f(fg_soft, fg_soft, ACT.Exp, scale=-1.0).then_inc(fg_act, 1)
                    act.wait_ge(fg_act, 1)
                    f(fg_soft, fg_soft, ACT.Ln, bias=1.0).then_inc(fg_act, 1)
                    split(n + 2)
                    f(tmp_r[0], fg_one, ACT.Copy).then_inc(fg_act, 1)
                    act.wait_ge(fg_step, 7)
                    f(tmp_r[3], tmp_r[1].bitcast(F32), ACT.Copy, scale=-1.0).then_inc(fg_act, 1)
                    f(tmp_r[4], tmp_r[2].bitcast(F32), ACT.Copy, scale=-1.0).then_inc(fg_act, 1)
                for c in range(1 + L, JV):
                    if c != 4:
                        split(n + c + 1)
                    if c == 3:
                        split(n + 5)
                    if c == 4:
                        if L == 0:
                            inverse_rms(stage, True, 0)
                        act.wait_ge(col_ready, L + 1)
                        act.wait_ge(job_done, n + 4)
                        for t in range(NT):
                            f(v32[:, t, 0:T], vb[0][t][:], ACT.Copy, scale=rms_col[:, t:t + 1]).then_inc(v_ready, 1)
                act.wait_ge(job_done, n + JV)
                for t in range(NT):
                    f(v32[:, t, T:D], vb[1][t][:], ACT.Copy, scale=rms_col[:, t:t + 1]).then_inc(v_ready, 1)
                for t in range(1, 4):
                    split(fq + t)
                act.wait_ge(v_ready, (2 * L + 2) * NT)
                if L == 0:
                    pair(0, "stick", 0)
                    loop(act, 1, STICK, lambda j: pair(0, "stick", j, "stick"))
                    pair(0, "dil", STICK, "stick")
                    loop(act, STICK + 1, NPAIR - 1, lambda j: pair(0, "dil", j, "dil"))
                    pair(0, "dil", NPAIR - 1, "dil", splits=False)
                else:
                    pair(1, "fox", 0)
                    loop(act, 1, NPAIR - 1, lambda j: pair(1, "fox", j, "fox"))
                    pair(1, "fox", NPAIR - 1, "fox", splits=False)
                finish("fox", (L + 1) * HEADS - 1, 1)
                for e in range(2):
                    heads_out((L + 1) * HEADS - 2 + e, e, blk(NPAIR - 1))

                def tail(stage, m, e):
                    act.wait_ge(x_new, m + ((stage - 1) * NB + 1))
                    alone()
                    gained(stage, m, e)
                    squares(stage, m, e)

                nj = out_job(L)

                def out_tiles(i, first=False):
                    for e in range(2):
                        if not (first and e == 0):
                            split(nj + e + 1, i * 2, i)
                        tail(stage + 1, i * 2 + e, e)
                out_tiles(0, first=True)
                loop(act, 1, NB // 2, out_tiles)

                nj = ffn_job(L)

                def in_tile(i, first=False):
                    split(nj + 1, i * 2, i)
                    if first:
                        inverse_rms(stage + 1, False, 3 * L + 2)
                        nc.scalar.preload_act_table_set("sigmoid_and_others")
                    act.wait_ge(g_scaled, i + (L * NF + 1))
                    f(f_sig, f_gate, ACT.Sigmoid).then_inc(g_sig, 1)
                    split(nj + 2, i * 2, i)
                    act.wait_ge(act_ready, i + (L * NF + 1))
                    alone()
                    f(f_hi[:].rearrange("p (c t) -> p c t", c=NF)[:, blk(i), :], tmp[:], ACT.Copy).then_inc(f_hi_ready, 1)
                in_tile(0, first=True)
                loop(act, 1, NF, in_tile)

                nj = ffn_out_job(L)

                def ffn_tiles(i, last=False):
                    for e in range(2):
                        for c in range(NOUT):
                            k = NOUT * e + c + 1
                            if last and L == DEPTH - 1 and k == 2 * NOUT:
                                break
                            a, b = OUT_CHUNKS[k % NOUT]
                            if last and k == 2 * NOUT:
                                split(g_job, view=gate_cols)
                            else:
                                split(nj + k, i * 6, i * 3, (b - a) * P)
                        tail(stage + 2, i * 2 + e, e)
                loop(act, 0, NB // 2 - 1, ffn_tiles)
                ffn_tiles(NB // 2 - 1, last=True)
            nc.scalar.preload_act_table_set("natural_log_exp_and_others")
            inverse_rms(2 * DEPTH, False, 3 * DEPTH)

        @block.vector
        def _(dve):
            v = nc.vector

            def split(n0, di=0, width=JOB, view=None):
                s = n0 % 2
                dve.wait_ge(w_hi_ready, di + (n0 + 1))
                view = view or (lambda w: w[:, s, 0:width])
                v.tensor_tensor(view(w_lo), view(w_raw), view(w_hi).bitcast(F32), ALU.subtract).then_inc(w_lo_ready, 1)

            def gained(stage, m):
                dve.wait_ge(h_hi_ready, m + (stage * NB + 1))
                v.scalar_tensor_tensor(h_lo[:, blk(m), :], x[:, blk(m), :], gains[:, stage, blk(m)],
                                       h_hi[:, blk(m), :].bitcast(F32), ALU.mult, ALU.subtract).then_inc(h_lo_ready, 1)

            def refine(stage, cols):
                dve.wait_ge(rms_raw, stage + 1)
                done = [newtons[0]]

                def step(ins):
                    done[0] += 1
                    ins.then_inc(newton, 1)
                    dve.wait_ge(newton, done[0])

                def steps(y, sums, t):
                    step(v.tensor_tensor(t, y, y, ALU.mult))
                    step(v.scalar_tensor_tensor(t, sums, D * EPS, t, ALU.add, ALU.mult))
                    step(v.tensor_scalar(t, t, -0.5 / D, 1.5, ALU.mult, ALU.add))
                    return v.tensor_tensor(y, y, t, ALU.mult)
                if cols:
                    steps(rms_col[:], col_sums[:, 0:NT], col_tmp[:]).then_inc(col_ready, 1)
                steps(rms[:], sums[:], tmp3[:]).then_inc(rms_ready, 1)
                newtons[0] = done[0]
                dve.wait_ge(rms_ready, stage + 1)

            newtons = [0]

            def scaled(L, kind, j, e, src=pb, alone=True):
                dve.wait_ge(job_done, j * 2 + (first_qk_job(L) + e + 1))
                sc, to = ((SCALE, tmp), (1.0, tmp2))[e]
                if kind == "dil":
                    r = (j - STICK) * 2 + e
                    v.scalar_tensor_tensor(to[:], src[:], sc, cosr[:], ALU.mult, ALU.mult)
                    v.stream_shuffle(tmp3[:], src[:], SWAP).then_inc(rope_shuffled, 1)
                    if alone:
                        dve.wait_ge(rope_shuffled, r + 1)
                        v.scalar_tensor_tensor(tmp3[:], tmp3[:], sc, sinr[:], ALU.mult, ALU.mult).then_inc(rope_sin, 1)
                        dve.wait_ge(rope_sin, r + 1)
                        v.tensor_tensor(to[:], to[:], tmp3[:], ALU.add).then_inc(qk_scaled, 1)
                else:
                    v.scalar_tensor_tensor(to[:], src[:], sc, rms[:], ALU.mult, ALU.mult).then_inc(qk_scaled, 1)

            def lo_part(to, x, hi):
                return v.tensor_tensor(to, x, hi, ALU.subtract)

            def heads_out(S, e, at):
                dve.wait_ge(o_hi_ready, S + 1)
                r = slice(DH * e, DH * (e + 1))
                v.tensor_tensor(o_lo[r, at, :], ob[r, :], o_hi[r, at, :].bitcast(F32), ALU.subtract).then_inc(o_lo_ready, 1)

            def finish(kind, S, e):
                for n, b in enumerate(KR):
                    c = slice(KO[b], KO[b] + KW[b])
                    hi, lo = pt[e]
                    if kind == "stick":
                        dve.wait_ge(stick_exp, S * NT + (n + 1))
                        v.tensor_copy(hi[:, c], s32[e][:, c]).then_inc(a_hi_ready, 1)
                    else:
                        dve.wait_ge(pt_hi_ready, (S - 2 * STICK) * NT + PASSED[n])
                        v.tensor_tensor(lo[:, c], zt(e, KW[b]), hi[:, c].bitcast(F32), ALU.subtract).then_inc(pt_lo_ready, 1)

            def pair(L, kind, j, next_kind, before=None, splits=True):
                for e in range(2):
                    S = j * 2 + (L * HEADS + e)
                    X = S - 2 * STICK
                    buf = s32[e]
                    if next_kind:
                        dve.wait_ge(qk_lo_ready, j * 4 + (4 * L * NPAIR + 4))
                        if next_kind == kind == "dil":
                            dve.wait_ge(qk_scaled, j * 2 + (2 + e))
                        scaled(L, next_kind, j + 1, e, alone=kind == "stick")
                    if before:
                        heads_out(S - 2, e, blk(j - 1))
                    if e == 1:
                        dve.wait_ge(vs_hi_ready, j + (L * NPAIR + 1))
                        v.tensor_tensor(v_lo[:], v32[:, :, bass.ds(j * P, P)], v_hi[:].bitcast(F32), ALU.subtract).then_inc(vs_ready, 1)
                    if kind != "stick":
                        for n, b in enumerate(QR):
                            dve.wait_ge(z_ready, S * NT + DONE[n])
                            v.tensor_reduce(nmax[:, b:b + 1], zt(e, QW[b]), AX, ALU.max, negate=True).then_inc(max_ready, 1)
                    if kind == "stick":
                        pieces(dve, v.tensor_copy, lo_part, v.tensor_copy, L, next_kind, j + 1, range(1, 4) if e else range(1))
                    if before or e == 1:
                        finish(before if e == 0 else kind, S - 1, 1 - e)
                    if kind != "stick" and next_kind:
                        pieces(dve, None, None, v.tensor_copy, L, next_kind, j + 1, range(1, 4) if e else range(1))
                    if splits and kind == "stick":
                        split(first_qk_job(L) + 4 + e, j * 2)
                    if kind == "stick":
                        if before or e == 1:
                            dve.wait_ge(second_ready, S * NT)

                        def high(n):
                            b = KR[n]
                            dve.wait_ge(sp_ready, S * NT + (n + 1))
                            c = slice(KO[b], KO[b] + KW[b])
                            v.tensor_copy(sp_hi[:, c], buf[:, c]).then_inc(sp_hi_ready, 1)
                        for n, b in enumerate(KR):
                            dve.wait_ge(ln_ready, S * NT + (n + 1))
                            c = slice(KO[b], KO[b] + KW[b])
                            v.scalar_tensor_tensor(buf[:, c], zt(e, KW[b]), 0.0, buf[:, c], ALU.max, ALU.add).then_inc(sp_ready, 1)
                            if n:
                                high(n - 1)
                        high(NT - 1)
                    else:
                        for n, b in enumerate(QR):
                            dve.wait_ge(rows_exp, X * NT + (n + 1))
                            c = slice(QO[b], QO[b] + QW[b])
                            if kind == "dil":
                                v.scalar_tensor_tensor(buf[:, c], buf[:, c], 1.0, mult[:, T - QW[b]:T], ALU.mult, ALU.mult,
                                                       accum_out=rsum[:, b:b + 1]).then_inc(rows_mult, 1)
                        if kind == "dil":
                            dve.wait_ge(rows_mult, X * NT + NT)
                        v.reciprocal(rinv[:], rsum[:]).then_inc(rows_inv, 1)
                        if kind == "fox":
                            dve.wait_ge(rows_inv, X + 1)
                        for b in range(NT) if kind == "fox" else ():
                            c = slice(QO[b], QO[b] + QW[b])
                            v.tensor_scalar(buf[:, c], buf[:, c], rinv[:, b:b + 1], None, ALU.mult).then_inc(rows_ready, 1)

            v.memset(eps[:], EPS).then_inc(eps_ready, 1)
            for e in range(2):
                last = v.memset(mv2[e][other(e), :].bitcast(F32), 0.0)
            last.then_inc(mv2_clear, 1)
            v.memset(ones[:], 1.0).then_inc(ones_ready, 1)
            dve.wait_ge(gains_loaded, 16)
            for m in range(NB):
                gained(0, m)
                if m < 2:
                    split(m)
            for L in range(DEPTH):
                stage = 2 * L
                n = JOB0[L] + L
                fq = first_qk_job(L)
                if L == 1:
                    v.memset(fg_one, 1.0).then_inc(ones_ready, 1)
                    split(n)
                    refine(stage, True)
                    dve.wait_ge(job_done, g_job + 1)
                    v.tensor_tensor(fg_z, logits[0:HEADS, :], rms[0:HEADS, :], ALU.mult).then_inc(fg_step, 1)
                    dve.wait_ge(fg_step, 1)
                    v.tensor_scalar(fg_z, fg_z, bforget[:], None, ALU.add).then_inc(fg_step, 1)
                    dve.wait_ge(fg_step, 2)
                    v.scalar_tensor_tensor(fg_soft, fg_z, -1.0, fg_z, ALU.mult, ALU.max).then_inc(fg_step, 1)
                    split(n + 1)
                    dve.wait_ge(fg_act, 2)
                    v.scalar_tensor_tensor(fg_z, fg_z, 0.0, fg_soft, ALU.min, ALU.subtract).then_inc(fg_step, 1)
                    split(n + 2)
                    dve.wait_ge(fg_step, 4)
                    v.tensor_tensor_scan(fg_sum, fg_one, fg_z, 0.0, ALU.mult, ALU.add).then_inc(fg_step, 1)
                    dve.wait_ge(fg_step, 5)
                    v.tensor_copy(tmp_r[1], fg_sum).then_inc(fg_step, 1)
                    dve.wait_ge(fg_step, 6)
                    v.tensor_tensor(tmp_r[2], fg_sum, tmp_r[1].bitcast(F32), ALU.subtract).then_inc(fg_step, 1)
                for c in range(1 + L, JV):
                    if c != 4:
                        split(n + c + 1)
                    if c == 3:
                        split(n + 5)
                    if c == 4 and L == 0:
                        refine(stage, True)
                        dve.wait_ge(const_loaded, 16 * 5)
                        v.tensor_tensor(cosr[:], cosr[:], rms[:], ALU.mult).then_inc(rope_ready, 1)
                        v.tensor_tensor(sinr[:], sinr[:], rms[:], ALU.mult).then_inc(rope_ready, 1)
                        dve.wait_ge(rope_ready, 2)
                        v.tensor_scalar(sin_q, sinr[:], SCALE, None, ALU.mult).then_inc(rope_ready, 1)
                kind = ("stick", "fox")[L]
                split(fq + 1)
                scaled(L, kind, 0, 0)
                split(fq + 2)
                scaled(L, kind, 0, 1, src=ob)
                pieces(dve, v.tensor_copy, lo_part, v.tensor_copy, L, kind, 0, range(4))
                split(fq + 3)
                if L == 0:
                    pair(0, "stick", 0, "stick")
                    loop(dve, 1, STICK - 1, lambda j: pair(0, "stick", j, "stick", "stick"))
                    pair(0, "stick", STICK - 1, "dil", "stick")
                    pair(0, "dil", STICK, "dil", "stick")
                    loop(dve, STICK + 1, NPAIR - 1, lambda j: pair(0, "dil", j, "dil", "dil"))
                    pair(0, "dil", NPAIR - 1, None, "dil", splits=False)
                else:
                    pair(1, "fox", 0, "fox")
                    loop(dve, 1, NPAIR - 1, lambda j: pair(1, "fox", j, "fox", "fox"))
                    pair(1, "fox", NPAIR - 1, None, "fox", splits=False)
                finish("fox", (L + 1) * HEADS - 1, 1)
                for e in range(2):
                    heads_out((L + 1) * HEADS - 2 + e, e, blk(NPAIR - 1))

                def tail(stage, m, e, done, di):
                    dve.wait_ge(job_done, di + (done + 1))
                    v.tensor_tensor(x[:, blk(m), :], x[:, blk(m), :], outs[e][:], ALU.add).then_inc(x_new, 1)
                    if stage < 2 * DEPTH:
                        gained(stage, m)

                nj = out_job(L)

                def out_tiles(i, first=False):
                    for e in range(2):
                        if not (first and e == 0):
                            if first:
                                dve.wait_ge(w_lo_ready, nj + 2)
                            split(nj + e + 1, i * 2)
                        tail(stage + 1, i * 2 + e, e, nj + e, i * 2)
                out_tiles(0, first=True)
                loop(dve, 1, NB // 2, out_tiles)

                nj = ffn_job(L)

                def in_tile(i, first=False):
                    t = i + L * NF
                    split(nj + 1, i * 2)
                    if first:
                        refine(stage + 1, False)
                    dve.wait_ge(job_done, i * 2 + (nj + 1))
                    v.tensor_tensor(f_gate, gate[:], rms[:], ALU.mult).then_inc(g_scaled, 1)
                    split(nj + 2, i * 2)
                    dve.wait_ge(g_sig, t + 1)
                    v.tensor_tensor(f_silu, f_gate, f_sig, ALU.mult).then_inc(g_silu, 1)
                    dve.wait_ge(job_done, i * 2 + (nj + 2))
                    v.tensor_tensor(f_up, up[:], rms[:], ALU.mult).then_inc(u_scaled, 1)
                    dve.wait_ge(u_scaled, t + 1)
                    if not (first and L == 0):
                        dve.wait_ge(f_lo_ready, t)
                    v.tensor_tensor(tmp[:], f_silu, f_up, ALU.mult).then_inc(act_ready, 1)
                    dve.wait_ge(f_hi_ready, t + 1)
                    v.tensor_tensor(f_lo[:].rearrange("p (c t) -> p c t", c=NF)[:, blk(i), :], tmp[:],
                                    f_hi[:].rearrange("p (c t) -> p c t", c=NF)[:, blk(i), :].bitcast(F32),
                                    ALU.subtract).then_inc(f_lo_ready, 1)
                in_tile(0, first=True)
                loop(dve, 1, NF, in_tile)

                nj = ffn_out_job(L)

                def ffn_tiles(i, last=False):
                    for e in range(2):
                        for c in range(NOUT):
                            k = NOUT * e + c + 1
                            if last and L == DEPTH - 1 and k == 2 * NOUT:
                                break
                            a, b = OUT_CHUNKS[k % NOUT]
                            if last and k == 2 * NOUT:
                                split(g_job, view=gate_cols)
                            else:
                                split(nj + k, i * 6, (b - a) * P)
                        tail(stage + 2, i * 2 + e, e, nj + NOUT * e + 2, i * 6)
                loop(dve, 0, NB // 2 - 1, ffn_tiles)
                ffn_tiles(NB // 2 - 1, last=True)
            refine(2 * DEPTH, False)
            for m in range(NB):
                v.tensor_tensor(y32[:, m, :], y32[:, m, :], rms[:], ALU.mult).then_inc(out_ready, 1)

        @block.gpsimd
        def _(pool):
            g = nc.gpsimd

            def squares(stage, m, e, first=False):
                pool.wait_ge(sq_ready, m + (stage * NB + 1))
                sq = (tmp, tmp2)[e][:]
                if first:
                    if stage:
                        pool.wait_ge(ssq_summed, stage)
                    g.tensor_copy(ssq[:], sq).then_inc(ssq_ready, 1)
                else:
                    pool.wait_ge(ssq_ready, m + stage * NB)
                    g.tensor_tensor(ssq[:], ssq[:], sq, ALU.add).then_inc(ssq_ready, 1)

            def stage_squares(stage):
                def two(i, first=False):
                    for e in range(2):
                        squares(stage, i * 2 + e, e, first and e == 0)
                two(0, first=True)
                loop(pool, 1, NB // 2, two)

            def low(S, e, ready, hi, lo, done):
                for n, b in enumerate(KR):
                    pool.wait_ge(ready, S * NT + (n + 1))
                    c = slice(KO[b], KO[b] + KW[b])
                    g.tensor_tensor(lo[:, c], s32[e][:, c], hi[:, c].bitcast(F32), ALU.subtract).then_inc(done, 1)

            def weights(S, e):
                low(S, e, a_hi_ready, *pt[e], a_lo_ready)

            def stick_pair(j, first=False):
                for e in range(2):
                    S = j * 2 + e
                    if not (first and e == 0):
                        weights(S - 1, 1 - e)
                    low(S, e, sp_hi_ready, sp_hi, sp_lo, sp_lo_ready)

            def lo_part(to, x, hi):
                return g.tensor_tensor(to, x, hi, ALU.subtract)

            def softmax_pair(L, kind, j, finish=False):
                for e in range(2):
                    if kind == "dil":
                        r = (j - STICK) * 2 + (2 + e)
                        pool.wait_ge(rope_shuffled, r + 1)
                        g.tensor_tensor(tmp3[:], tmp3[:], (sin_q, sinr[:])[e], ALU.mult).then_inc(rope_sin, 1)
                        pool.wait_ge(rope_sin, r + 1)
                        to = (tmp, tmp2)[e]
                        g.tensor_tensor(to[:], to[:], tmp3[:], ALU.add).then_inc(qk_scaled, 1)
                    if finish and e == 0:
                        weights(2 * STICK - 1, 1)
                        pool.wait_ge(a_lo_ready, 2 * STICK * NT)
                    elif kind == "dil":
                        pool.wait_ge(qk_scaled, j * 2 + (3 + e))
                    for i in (range(1, 4) if e else range(1)):
                        if i:
                            pool.wait_ge(qk_lo_ready, j * 4 + (4 * L * NPAIR + 4 + i))
                        pieces(pool, None, lo_part, None, L, kind, j + 1, range(i, i + 1))
                    pool.wait_ge(qk_lo_ready, j * 4 + (4 * L * NPAIR + 5 + (3 if e else 0)))
                    n0 = first_qk_job(L) + 4 + e
                    s = n0 % 2
                    pool.wait_ge(w_hi_ready, j * 2 + (n0 + 1))
                    pool.wait_ge(w_lo_ready, j * 2 + n0)
                    g.tensor_tensor(w_lo[:, s], w_raw[:, s], w_hi[:, s].bitcast(F32), ALU.subtract).then_inc(w_lo_ready, 1)
                    pool.wait_ge(w_lo_ready, j * 2 + (n0 + 1))

            stage_squares(0)
            stick_pair(0, first=True)
            loop(pool, 1, STICK, stick_pair)
            pool.wait_ge(rope_ready, 3)
            softmax_pair(0, "dil", STICK, finish=True)
            loop(pool, STICK + 1, NPAIR - 1, lambda j: softmax_pair(0, "dil", j))
            for stage in range(1, 2 * DEPTH + 1):
                stage_squares(stage)
                if stage == 2:
                    pool.wait_ge(job_done, JOB0[1])
                    pool.wait_ge(ssq_ready, 3 * NB)
                    for side, rows in enumerate((st2[0], mv2[0], st2[1], mv2[1])):
                        if side == 2:
                            pool.wait_ge(rows_clear, 2)
                        g.memset(rows[other(side // 2), :].bitcast(F32), 0.0).then_inc(rows_clear, 1)
                    pool.wait_ge(rows_clear, 4)
                    loop(pool, 0, NPAIR - 1, lambda j: softmax_pair(1, "fox", j))


def _tables():
    q = np.arange(P)[:, None]
    k = np.arange(T)[None, :] - (T - P)
    dist = q - k
    mult = ((dist >= 0) & (dist <= 128)).astype(np.float32)
    mult += (dist >= 0) & (dist % 4 == 0)
    mult += (dist >= 0) & (dist % 16 == 0)
    dil = np.where(mult > 0, 0.0, MASKED)
    r = np.arange(P)
    causal = np.where(r[None, :] <= r[:, None], 0.0, MASKED)
    strict = np.where(r[:, None] < r[None, :], 0.0, MASKED)
    tri = np.where(r[:, None] >= r[None, :], -1.0, 0.0)
    masks = np.concatenate([dil, causal, strict, np.eye(P), tri], 1).astype(np.float32)
    half = ROT // 2
    inv = (np.float32(THETA) ** (-np.arange(half, dtype=np.float32) * np.float32(2.0) / np.float32(ROT))).astype(np.float32)
    ang = np.arange(T, dtype=np.float32)[None, :] * inv[:, None]
    cos, sin = np.cos(ang), np.sin(ang)
    rope = np.zeros((2, P, T), np.float32)
    rope[0] = 1.0
    for h in (0, DH):
        rope[0, h:h + half] = rope[0, h + half:h + ROT] = cos
        rope[1, h:h + half], rope[1, h + half:h + ROT] = -sin, sin
    return rope, mult.astype(np.float32), masks


def _tiles(w):
    k, n = w.shape
    return w.reshape(k // P, P, n // P, P).transpose(2, 1, 0, 3).reshape(n // P, P, k)


def _attention_jobs(w, w_o):
    q, k, v = w[:, 0:D], w[:, D:2 * D], w[:, 2 * D:3 * D]
    vj = v.reshape(4, 2, P, 2, T).transpose(3, 0, 2, 1, 4).reshape(JV, P, JOB)
    qk = np.stack([_tiles(q), _tiles(k)], 1).reshape(JQK, P, JOB)
    return np.ascontiguousarray(np.concatenate([vj, qk, _tiles(w_o)], 0))


def kernel(x, norm_mix, w_qkv_even, w_o_even, w_qkvf_odd, b_forget, w_o_odd, norm_ffn, w_ffn_in, w_ffn_out, norm_final):
    import concourse.bacc as _bacc
    from concourse.bass_utils import run_bass_kernel_spmd as _run

    a = np.asarray
    xt = a(x)[0].T.reshape(NB, P, T).transpose(1, 0, 2)
    gains = np.stack([a(norm_mix)[0], a(norm_ffn)[0], a(norm_mix)[1], a(norm_ffn)[1], a(norm_final)], 0)
    wf = a(w_qkvf_odd)[0][:, 3 * D:].reshape(NB, P, HEADS).transpose(1, 0, 2)
    win = np.stack([np.stack([_tiles(w[:, :DFF]), _tiles(w[:, DFF:])], 1).reshape(JIN, P, D) for w in a(w_ffn_in)])
    wout = np.stack([_tiles(w) for w in a(w_ffn_out)])
    rope, mult, masks = _tables()
    arrays = {
        "xt": xt, "gains": gains.reshape(2 * DEPTH + 1, NB, P).transpose(2, 0, 1),
        "wa0": _attention_jobs(a(w_qkv_even)[0], a(w_o_even)[0]),
        "wa1": _attention_jobs(a(w_qkvf_odd)[0], a(w_o_odd)[0]),
        "wf": wf, "win": win, "wout": wout, "bf": a(b_forget)[0][:, None],
        "rope": rope, "mult": mult, "masks": masks,
    }
    nc = _bacc.Bacc("TRN2", target_bir_lowering=False, num_devices=1)
    feed, args = {}, []
    for name, v in arrays.items():
        v = np.ascontiguousarray(v)
        feed[f"in_{name}"] = v
        args.append(nc.dram_tensor(f"in_{name}", v.shape, mybir.dt.from_np(v.dtype), kind="ExternalInput").ap())
    args.append(nc.dram_tensor("out_t", (P, NB, T), F32, kind="ExternalOutput").ap())
    trunk(nc, *args)
    r = _run(nc, [feed], core_ids=[0])
    out = r.results[0]["out_t"]
    return np.ascontiguousarray(out.transpose(2, 1, 0).reshape(T, D))[None]
```

```python
from contextlib import ExitStack

import numpy as np
import concourse.bass as bass
from concourse import mybir

F32 = mybir.dt.float32
F32R = mybir.dt.float32r
BF16 = mybir.dt.bfloat16
ALU = mybir.AluOpType
ACT = mybir.ActivationFunctionType
AX = mybir.AxisListType.X

P = 128
D, T, DH, DFF, DEPTH = 1024, 512, 64, 2816, 2
NB = D // P
NT = T // P
NF = DFF // P
NPAIR = D // (2 * DH)
HEADS = 2 * NPAIR
STICK = NPAIR // 2
SCALE = DH ** -0.5
EPS = 1e-5
THETA = 500000.0
ROT = DH // 4
CONSTS = 7
MASKED = -1e30
POOL_OUT = 2
JOB = 8 * P
X_LOADS = [(0, 1), (1, 2), (2, 4), (4, 6), (6, 8)]

KW = [T - b * P for b in range(NT)]
KO = [sum(KW[:b]) for b in range(NT)]
QW = [(b + 1) * P for b in range(NT)]
QO = [sum(QW[:b]) for b in range(NT)]
TRI = sum(KW)
PACK = {4 * P: (0, 0), 3 * P: (1, 0), P: (1, 3 * P), 2 * P: (2, 0)}
KR, QR = (2, 3, 1, 0), (1, 0, 2, 3)
SIGNALS, DONE, PASSED = 3, (1, 2, 2, 3), (1, 3, 3, 4)

JV, JQK, JO, JIN, NOUT = 8, 2 * NPAIR, NB, 2 * NF, 3
OUT_CHUNKS = [(0, 8), (8, 15), (15, 22)]
JATT = [JV + JQK + JO, JV + 1 + JQK + JO]
FILL = [(range(0, 2),), (range(2, 5), range(5, 7))]
JOB0 = [0, JATT[0] + JIN + NOUT * NB]
SWAP = [(i + ROT // 2) % ROT if i < ROT else i for i in range(32)]


def loop(eng, start, end, body):
    if end - start == 1:
        body(start)
    elif end > start:
        with eng.Fori(start, end) as i:
            body(i)


def blk(i):
    return bass.ds(i, 1)


def trunk(nc, xt_d, gains_d, wa0_d, wa1_d, wf_d, win_d, wout_d, bf_d, rope_d, mult_d, masks_d, out_d):
    ctx = ExitStack()
    with ctx:
        def sb(name, shape, dt=F32):
            return ctx.enter_context(nc.sbuf_tensor(name, shape, dt))

        def bank(name):
            return ctx.enter_context(nc.psum_tensor(name, [P, T], F32))

        def sem(name):
            return ctx.enter_context(nc.semaphore(name))

        x = sb("x", [P, NB, T])
        h_hi = sb("h_hi", [P, NB, T], F32R)
        h_lo = sb("h_lo", [P, NB, T], F32R)
        w_raw = sb("w_raw", [P, 2, JOB])
        w_hi = sb("w_hi", [P, 2, JOB], F32R)
        w_lo = sb("w_lo", [P, 2, JOB], F32R)
        f_hi = sb("f_hi", [P, NF * T], F32R)
        f_lo = sb("f_lo", [P, NF * T], F32R)

        used = [0]

        def parts(n, *shape):
            a, used[0] = used[0], used[0] + n
            assert used[0] <= NF * T
            return f_hi[:, a:a + n], f_lo[:, a:a + n]

        o_hi, o_lo = (v.rearrange("p (c t) -> p c t", c=NB) for v in parts(NB * T))
        pt = [parts(TRI) for _ in range(2)]
        sp_hi, sp_lo = parts(TRI)
        st, mv, mv2, st2 = (parts(T) for _ in range(4))
        v_hi, v_lo = (v.rearrange("p (c t) -> p c t", c=NT) for v in parts(NT * P))
        neg_tri, neg_one = parts(P)

        v32 = sb("v32", [P, NT, D])
        s32 = [sb(f"s32_{i}", [P, TRI]) for i in range(2)]
        tmp = sb("tmp", [P, T])
        tmp2 = sb("tmp2", [P, T])
        tmp3 = sb("tmp3", [P, T])
        col_tmp = sb("col_tmp", [P, NT])
        rms = sb("rms", [P, T])
        rms_col = sb("rms_col", [P, NT])
        cosr = sb("cosr", [P, T])
        sinr = sb("sinr", [P, T])
        mult = sb("mult", [P, T])
        ssq = sb("ssq", [P, T])
        ones = sb("ones", [P, P])
        ident = sb("ident", [P, P])
        ident_b = sb("ident_b", [P, P], BF16)
        m_dil = sb("m_dil", [P, T], BF16)
        m_causal = sb("m_causal", [P, P], BF16)
        m_strict = sb("m_strict", [P, P], BF16)
        gains = sb("gains", [P, 2 * DEPTH + 1, NB])
        bforget = sb("bforget", [HEADS, 1])
        eps = sb("eps", [P, 1])
        nmax = sb("nmax", [P, NT])
        rsum = sb("rsum", [P, NT])
        rinv = sb("rinv", [P, NT])
        f_rows = nc.dram_tensor("f_rows", (2, 4, HEADS, T), F32).ap()
        masks32 = v32[:, 0, :]

        zb = [[bank(f"zb{e}{b}") for b in range(3)] for e in range(2)]
        pb = bank("pb")
        ob = bank("ob")
        sums, col_sums = ob, zb[1][2]
        gate, up = (zb[1][0], zb[0][1]), (zb[1][1], zb[0][2])
        outs = [pb, zb[0][0]]
        vb = [[*zb[0], zb[1][0]], [zb[1][1], pb, sums, col_sums]]
        logits = vb[1][0]
        first_tiles = [zb[0][0], zb[0][1], pb]

        def zt(e, w):
            b, at = PACK[w]
            return zb[e][b][:, at:at + w]

        x_loaded = [sem(f"x_loaded{i}") for i in range(len(X_LOADS))]
        start_loaded, start_hi_ready, start_lo_ready = sem("start_loaded"), sem("start_hi_ready"), sem("start_lo_ready")
        gains_loaded, const_loaded, const_ready, ones_ready = (sem(n) for n in ("gains_loaded", "const_loaded", "const_ready", "ones_ready"))
        w_loaded = [sem("w_loaded0"), sem("w_loaded1")]
        w_hi_ready, w_lo_ready, job_done = sem("w_hi_ready"), sem("w_lo_ready"), sem("job_done")
        h_hi_ready, h_lo_ready, x_new = sem("h_hi_ready"), sem("h_lo_ready"), sem("x_new")
        sq_ready, ssq_ready, ssq_summed, ln_done, rms_ready = (sem(n) for n in ("sq_ready", "ssq_ready", "ssq_summed", "ln_done", "rms_ready"))
        v_ready = sem("v_ready")
        qk_scaled, qk_hi_ready, qk_lo_ready, qk_dup_ready = (sem(n) for n in ("qk_scaled", "qk_hi_ready", "qk_lo_ready", "qk_dup_ready"))
        vs_hi_ready, vs_ready = sem("vs_hi_ready"), sem("vs_ready")
        z_ready, abs_ready, exp_done, ln_ready = (sem(n) for n in ("z_ready", "abs_ready", "exp_done", "ln_ready"))
        sp_ready, sp_hi_ready, sp_lo_ready = sem("sp_ready"), sem("sp_hi_ready"), sem("sp_lo_ready")
        max_ready, rows_exp, rows_mult, rows_inv, rows_ready = (sem(n) for n in ("max_ready", "rows_exp", "rows_mult", "rows_inv", "rows_ready"))
        a_hi_ready, a_lo_ready = sem("a_hi_ready"), sem("a_lo_ready")
        second_ready, stick_exp, pt_hi_ready, pt_lo_ready = (sem(n) for n in ("second_ready", "stick_exp", "pt_hi_ready", "pt_lo_ready"))
        o_summed, o_hi_ready, o_lo_ready = sem("o_summed"), sem("o_hi_ready"), sem("o_lo_ready")
        g_scaled, g_sig, g_silu, u_scaled, act_ready, f_hi_ready, f_lo_ready = (sem(n) for n in (
            "g_scaled", "g_sig", "g_silu", "u_scaled", "act_ready", "f_hi_ready", "f_lo_ready"))
        fg_step, fg_act, rows_stored, rows_loaded = (sem(n) for n in ("fg_step", "fg_act", "rows_stored", "rows_loaded"))
        eps_ready, col_ready, rms_raw, newton = sem("eps_ready"), sem("col_ready"), sem("rms_raw"), sem("newton")
        rows_clear, pool_out_ready = sem("rows_clear"), sem("pool_out_ready")
        rope_shuffled, rope_sin, mv2_clear = sem("rope_shuffled"), sem("rope_sin"), sem("mv2_clear")
        rope_ready, out_ready, out_stored = sem("rope_ready"), sem("out_ready"), sem("out_stored")

        f_gate, f_sig, f_silu, f_up = s32[0][:, 0:T], s32[0][:, T:2 * T], s32[1][:, 0:T], s32[1][:, T:2 * T]
        fg_z, fg_soft, fg_sum, fg_one = (v[0:HEADS, :] for v in (f_gate, f_sig, f_silu, f_up))
        sin_q = ssq[:]
        y32 = v32[:].rearrange("p a b -> p (a b)").rearrange("p (m t) -> p m t", m=NB)
        g_job = JOB0[1]

        def gate_cols(w):
            return w[:, g_job % 2, :].rearrange("p (c n) -> p c n", c=NB)[:, :, 0:HEADS]

        def second_half(w):
            return w[:, 0, T:JOB]

        tmp_r = [v[0:HEADS, :] for v in (sp_hi[:, 0:T], sp_hi[:, T:2 * T], sp_lo[:, 0:T], sp_lo[:, T:2 * T], pt[1][0][:, 0:T])]

        block = ctx.enter_context(nc.Block())

        def first_qk_job(L):
            return JOB0[L] + JV + L

        def out_job(L):
            return JOB0[L] + JATT[L] - JO

        def ffn_job(L):
            return JOB0[L] + JATT[L]

        def ffn_out_job(L):
            return ffn_job(L) + JIN

        def own(e):
            return slice(DH * e, DH * (e + 1))

        def other(e):
            return own(1 - e)

        def is_st(kind, i):
            return (i % 2 == 1) == (kind == "stick")

        def pieces(eng, f_hi_part, f_lo_part, f_dup, L, kind, jn, which):
            def tiles(i):
                e = i // 2
                return e, (tmp, tmp2)[i % 2], (st if is_st(kind, i) else mv)[e]
            if f_hi_part:
                for i in which:
                    e, t, to = tiles(i)
                    eng.wait_ge(qk_scaled, jn * 2 + (L * HEADS + 1 + i % 2))
                    if not isinstance(jn, int) or jn > 0:
                        eng.wait_ge(z_ready, jn * (2 * SIGNALS) + (L * HEADS + e - 1) * SIGNALS)
                    f_hi_part(to[own(e), :], t[own(e), :]).then_inc(qk_hi_ready, 1)
            if f_lo_part:
                for i in which:
                    e, t, hi = tiles(i)
                    eng.wait_ge(qk_hi_ready, jn * 4 + (4 * L * NPAIR + i + 1))
                    out = st[e][other(e), :] if is_st(kind, i) else mv2[e][own(e), :]
                    f_lo_part(out, t[own(e), :], hi[own(e), :].bitcast(F32)).then_inc(qk_lo_ready, 1)
            if f_dup:
                for i in which:
                    e, t, hi = tiles(i)
                    if not is_st(kind, i) or kind == "fox":
                        eng.wait_ge(qk_hi_ready, jn * 4 + (4 * L * NPAIR + i + 1))
                        out = st2[e][own(e), :] if is_st(kind, i) else mv[e][other(e), :]
                        f_dup(out, hi[own(e), :].bitcast(F32)).then_inc(qk_dup_ready, 1)

        @block.sync
        def _(sp):
            def load(n0, di, half, src, width=JOB):
                s = n0 % 2
                if n0 >= 2:
                    sp.wait_ge(w_hi_ready, di + (n0 - 1))
                    sp.wait_ge(w_lo_ready, di + (n0 - 1))
                sp.dma_start(w_raw[:, s, 0:width], src).then_inc(w_loaded[s], 16)

            def loads(n0, count, dram, first):
                def two(i):
                    for e in range(2):
                        load(n0 + e, i * 2, i, dram[blk(i * 2 + (first + e))].rearrange("o p n -> p (o n)"))
                loop(sp, 0, count // 2, two)

            sp.dma_start(gains[:], gains_d).then_inc(gains_loaded, 16)
            for i, (a, b) in enumerate(X_LOADS):
                sp.dma_start(x[:, a:b, :], xt_d[:, a:b, :]).then_inc(x_loaded[i], 16)
                if i == 0:
                    sp.dma_start(w_raw[:, 0, 0:T], wa0_d[0, :, 0:T]).then_inc(start_loaded, 16)
                elif i == 1:
                    sp.dma_start(w_raw[:, 0, T:JOB], wa0_d[0, :, T:JOB]).then_inc(w_loaded[0], 16)
                elif i == 2:
                    load(1, 0, 0, wa0_d[1])
            sp.dma_start(masks32, masks_d).then_inc(const_loaded, 16)
            sp.dma_start(cosr[:], rope_d[0]).then_inc(const_loaded, 16)
            sp.dma_start(sinr[:], rope_d[1]).then_inc(const_loaded, 16)
            sp.dma_start(mult[:], mult_d).then_inc(const_loaded, 16)
            sp.dma_start(bforget[:], bf_d).then_inc(const_loaded, 16)

            def f_load(j):
                for e in range(2):
                    for ab, rows in enumerate((st2[e], mv2[e])):
                        sp.dma_start(rows[DH * (1 - e):DH * (1 - e) + 4, :].bitcast(F32),
                                     f_rows[ab][:, blk(j * 2 + e), :].rearrange("r o t -> r (o t)")).then_inc(rows_loaded, 16)

            for L in range(DEPTH):
                n = JOB0[L]
                wa = (wa0_d, wa1_d)[L]
                if L == 0:
                    loads(2, JATT[0] - 2, wa, 2)
                else:
                    sp.wait_ge(w_hi_ready, g_job - 1)
                    sp.wait_ge(w_lo_ready, g_job - 1)
                    sp.dma_start(gate_cols(w_raw), wf_d).then_inc(w_loaded[g_job % 2], 16)
                    loads(n + 1, JV - 2, wa, 0)
                    sp.wait_ge(fg_step, 7)
                    sp.wait_ge(fg_act, 5)
                    one, hi, lo, nhi, nlo = (tmp_r[i] for i in range(5))
                    for ab, rows in enumerate(((one, one, hi, lo), (nhi, nlo, one, one))):
                        for r, src in enumerate(rows):
                            sp.dma_start(f_rows[ab, r], src.bitcast(F32)).then_inc(rows_stored, 16)
                    loads(n + 1 + JV - 2, 2, wa, JV - 2)
                    sp.wait_ge(rows_stored, 16 * 8)
                    sp.wait_ge(rows_clear, 4)
                    f_load(0)
                    for r in range(JV, JV + 5):
                        load(n + 1 + r, 0, 0, wa[r])

                    def pair(j):
                        for e in range(2):
                            r = JV + 5 + e
                            load(n + 1 + r, j * 2, j, wa[blk(j * 2 + r)].rearrange("o p n -> p (o n)"))
                        sp.wait_ge(z_ready, j * (2 * SIGNALS) + (HEADS + 2) * SIGNALS)
                        f_load(j + 1)
                    loop(sp, 0, NPAIR - 1, pair)
                    done = JV + 5 + 2 * (NPAIR - 1)
                    load(n + 1 + done, 0, 0, wa[done])
                    loads(n + 2 + done, JV + JQK + JO - done - 1, wa, done + 1)
                loads(ffn_job(L), JIN, win_d[L], 0)
                no = ffn_out_job(L)

                def two_tiles(i):
                    for e in range(2):
                        for c, (a, b) in enumerate(OUT_CHUNKS):
                            k = NOUT * e + c
                            load(no + k, i * 6, i * 3,
                                 wout_d[L][blk(i * 2 + e), :, a * P:b * P].rearrange("o p n -> p (o n)"), (b - a) * P)
                loop(sp, 0, NB // 2, two_tiles)

            for m in (0, 1, 2, NB - 2, 3, 4, 5, NB - 1):
                if m < NB - POOL_OUT:
                    sp.wait_ge(out_ready, m + 1)
                else:
                    sp.wait_ge(pool_out_ready, m + 1 - (NB - POOL_OUT))
                sp.dma_start(out_d[:, m, :], v32[:].rearrange("p a b -> p (a b)")[:, m * T:(m + 1) * T]).then_inc(out_stored, 16)
            sp.wait_ge(out_stored, 16 * NB)


        @block.tensor
        def _(pe):
            mm = nc.tensor.matmul

            def job_ready(n0, di):
                pe.wait_ge(w_hi_ready, di + (n0 + 1))
                pe.wait_ge(w_lo_ready, di + (n0 + 1))

            def product(out, s, chunks, hi, lo, start=True, stop=True, wait=None, at=0, ends=True):
                for c, k in enumerate(chunks, at):
                    if wait:
                        wait(k)
                    wh, wl = w_hi[:, s, c * P:(c + 1) * P], w_lo[:, s, c * P:(c + 1) * P]
                    mm(out, wh, hi[:, k, :], start=start and c == at, stop=False)
                    mm(out, wh, lo[:, k, :], start=False, stop=False)
                    last = mm(out, wl, hi[:, k, :], start=False, stop=stop and c == at + len(chunks) - 1)
                if ends:
                    last.then_inc(job_done, 1)

            def h_ready(stage):
                def wait(k):
                    pe.wait_ge(h_hi_ready, stage * NB + k + 1)
                    pe.wait_ge(h_lo_ready, stage * NB + k + 1)
                return wait

            def sum_squares(stage, cols):
                pe.wait_ge(ssq_ready, (stage + 1) * NB)
                last = mm(sums[:], ones[:], ssq[:], start=True, stop=True)
                if cols:
                    for t in range(NT):
                        last = mm(col_sums[:, t:t + 1], ssq[:, t * P:(t + 1) * P], ones[:, 0:1], start=True, stop=True)
                last.then_inc(ssq_summed, 1)

            def read(kind, S):
                if kind == "stick":
                    pe.wait_ge(stick_exp, S * NT + NT)
                else:
                    pe.wait_ge(pt_hi_ready, (S - 2 * STICK) * NT + NT)
                    pe.wait_ge(pt_lo_ready, (S - 2 * STICK) * NT + NT)

            def scores(kind, S, e):
                order = list(range(NT) if kind != "stick" else reversed(range(NT)))
                for b in order:
                    at, w, move = ((slice(b * P, (b + 1) * P), KW[b], slice(b * P, T)) if kind == "stick" else
                                   (slice(b * P, (b + 1) * P), QW[b], slice(0, QW[b])))
                    out = zt(e, w)
                    mm(out, st[e][:, at], mv[e][:, move], start=w != 3 * P, stop=False, skip_group_check=True)
                    mm(out, (st2 if kind == "fox" else st)[e][:, at], mv2[e][:, move], start=False, stop=False,
                       skip_group_check=True)
                for n, b in enumerate(order):
                    w = KW[b] if kind == "stick" else QW[b]
                    mask, at = ((m_strict[:], slice(0, P)) if kind == "stick" else
                                (m_dil[:, T - w:T], slice(0, w)) if kind == "dil" else (m_causal[:], slice(w - P, w)))
                    last = mm(zt(e, w)[:, at], ident_b[:], mask, start=False, stop=True, skip_group_check=True)
                    if n:
                        last.then_inc(z_ready, 1)

            def suffix_sums(S, e):
                pe.wait_ge(sp_hi_ready, S * NT + NT)
                pe.wait_ge(sp_lo_ready, S * NT + NT)
                for b in reversed(range(NT)):
                    out = zt(e, KW[b])
                    for later in range(b + 1, NT):
                        for v in (sp_hi, sp_lo):
                            mm(out[:, (later - b) * P:KW[b]], neg_one, v[:, KO[later]:KO[later] + KW[later]],
                               start=False, stop=False, skip_group_check=True)
                    for v in (sp_hi, sp_lo):
                        last = mm(out, neg_tri, v[:, KO[b]:KO[b] + KW[b]],
                                  start=False, stop=v is sp_lo, skip_group_check=True)
                    if b < NT - 1:
                        last.then_inc(second_ready, 1)

            def transposes(S, e):
                pe.wait_ge(rows_ready, (S - 2 * STICK) * NT + NT)
                for b in range(NT):
                    for k in reversed(range(b + 1)):
                        last = nc.tensor.transpose(zt(e, KW[k])[:, (b - k) * P:(b - k + 1) * P],
                                                   s32[e][:, QO[b] + k * P:QO[b] + (k + 1) * P], ident[:])
                        if b == NT - 1 and k in (2, 0):
                            last.then_inc(second_ready, 2 - k // 2)

            def second(kind, S, e):
                (suffix_sums if kind == "stick" else transposes)(S, e)

            def values(S, kind, e):
                hi, lo = pt[e]
                for n, b in enumerate(KR):
                    X = S if kind == "stick" else S - 2 * STICK
                    pe.wait_ge(a_hi_ready if kind == "stick" else pt_hi_ready, X * NT + (n + 1))
                    pe.wait_ge(a_lo_ready if kind == "stick" else pt_lo_ready, X * NT + (n + 1))
                    out, c = ob[:, b * P:T], slice(KO[b], KO[b] + KW[b])
                    mm(out, v_hi[:, b, :], hi[:, c], start=n == 0, stop=False, skip_group_check=True)
                    mm(out, v_hi[:, b, :], lo[:, c], start=False, stop=False, skip_group_check=True)
                    last = mm(out, v_lo[:, b, :], hi[:, c], start=False, stop=n == NT - 1, skip_group_check=True)
                last.then_inc(o_summed, 1)

            def out_part(L, n, blocks):
                def wait(k):
                    pe.wait_ge(o_hi_ready, L * HEADS + 2 * k + 2)
                    pe.wait_ge(o_lo_ready, L * HEADS + 2 * k + 2)
                job = out_job(L) + n
                job_ready(job, 0)
                product(outs[n][:], job % 2, blocks, o_hi, o_lo, start=blocks[0] == 0, stop=blocks[-1] == NB - 1, wait=wait,
                        at=blocks[0], ends=blocks[-1] == NB - 1)

            def pair(L, kind, j, before=None, projects=2, first=False, fill=(), ropes=False):
                for e in range(2):
                    S = j * 2 + (L * HEADS + e)
                    pe.wait_ge(qk_lo_ready, j * 4 + (4 * L * NPAIR + 2 * e + 2))
                    pe.wait_ge(qk_dup_ready, j * 4 + (2 * NPAIR + 2 * e + 2) if kind == "fox" else j * 2 + (e + 1))
                    if e == 0 and kind == "fox":
                        pe.wait_ge(rows_loaded, j * 64 + 64)
                    if not first:
                        read(before, S - 2)
                    scores(kind, S, e)
                    if not (first and e == 0):
                        second(before if e == 0 else kind, S - 1, 1 - e)
                    if e < projects:
                        n0 = first_qk_job(L) + 3 + e
                        job_ready(n0, j * 2)
                        if ropes:
                            pe.wait_ge(rope_shuffled, j * 2 + (3 + e - 2 * STICK))
                        else:
                            pe.wait_ge(qk_scaled, j * 2 + (L * HEADS + 3 + e))
                        product(pb[:], n0 % 2, range(NB), h_hi, h_lo)
                    elif fill:
                        if fill[0][0] == 0:
                            pe.wait_ge(qk_scaled, (L + 1) * HEADS)
                        out_part(L, 0, fill[e - projects])
                    if not (first and e == 0):
                        if not first:
                            pe.wait_ge(o_hi_ready, S - 1)
                            pe.wait_ge(o_lo_ready, S - 1)
                        if e == 1:
                            pe.wait_ge(vs_ready, j + (L * NPAIR + 1))
                        values(S - 1, before if e == 0 else kind, 1 - e)

            pe.wait_ge(ones_ready, 1)
            for L in range(DEPTH):
                stage = 2 * L
                n = JOB0[L] + L
                if L == 1:
                    job_ready(g_job, 0)
                    product(logits[:], g_job % 2, range(NB), h_hi, h_lo, wait=h_ready(stage))
                    sum_squares(stage, True)
                for half in range(2):
                    for c2 in range(4):
                        job = n + 4 * half + c2
                        s = job % 2
                        for c in range(2):
                            k = 2 * c2 + c
                            if job == 0 and c == 0:
                                pe.wait_ge(start_hi_ready, 1)
                                pe.wait_ge(start_lo_ready, 1)
                            elif c == 0 or job == 0:
                                job_ready(job, 0)
                            if half == 0:
                                h_ready(stage)(k)
                            wh, wl = w_hi[:, s, c * T:(c + 1) * T], w_lo[:, s, c * T:(c + 1) * T]
                            for t in range(NT):
                                out, tt = vb[half][t][:], slice(t * P, (t + 1) * P)
                                if half == 1 and k == 0 and t == 0 and L == 1:
                                    pe.wait_ge(fg_step, 1)
                                if half == 1 and k == 0 and t == 2:
                                    pe.wait_ge(rms_ready, stage + 1)
                                mm(out, h_hi[:, k, tt], wh, start=k == 0, stop=False)
                                mm(out, h_hi[:, k, tt], wl, start=False, stop=False)
                                last = mm(out, h_lo[:, k, tt], wh, start=False, stop=k == NB - 1)
                        last.then_inc(job_done, 1)
                        if half == 0 and c2 == 2 and L == 0:
                            sum_squares(stage, True)
                pe.wait_ge(v_ready, (2 * L + 1) * NT)
                for t in range(3):
                    n0 = first_qk_job(L) + t
                    job_ready(n0, 0)
                    if t == 2:
                        pe.wait_ge(v_ready, (2 * L + 2) * NT)
                    product(first_tiles[t][:], n0 % 2, range(NB), h_hi, h_lo)
                if L == 0:
                    pe.wait_ge(const_ready, CONSTS)
                    pe.wait_ge(mv2_clear, 1)
                    pair(0, "stick", 0, first=True)
                    loop(pe, 1, STICK - 1, lambda j: pair(0, "stick", j, "stick"))
                    pair(0, "stick", STICK - 1, "stick", ropes=True)
                    pair(0, "dil", STICK, "stick", ropes=True)
                    loop(pe, STICK + 1, NPAIR - 2, lambda j: pair(0, "dil", j, "dil", ropes=True))
                    pair(0, "dil", NPAIR - 2, "dil", projects=1, fill=FILL[0], ropes=True)
                    pair(0, "dil", NPAIR - 1, "dil", projects=0, fill=FILL[1])
                else:
                    pair(1, "fox", 0, first=True)
                    loop(pe, 1, NPAIR - 2, lambda j: pair(1, "fox", j, "fox"))
                    pair(1, "fox", NPAIR - 2, "fox", projects=1, fill=FILL[0])
                    pair(1, "fox", NPAIR - 1, "fox", projects=0, fill=FILL[1])
                S = (L + 1) * HEADS
                read("fox", S - 2)
                out_part(L, 1, range(0, 2))
                second("fox", S - 1, 1)
                out_part(L, 1, range(2, 5))
                pe.wait_ge(o_hi_ready, S - 1)
                pe.wait_ge(o_lo_ready, S - 1)
                values(S - 1, "fox", 1)
                out_part(L, 1, range(5, 6))
                out_part(L, 0, range(7, 8))
                out_part(L, 1, range(6, 8))

                def added(stage, i, e):
                    pe.wait_ge(x_new, i * 2 + ((stage - 1) * NB + e - 1))

                nj = out_job(L)

                def out_tiles(i):
                    for e in range(2):
                        added(stage + 1, i, e)
                        job_ready(nj + e, i * 2)
                        product(outs[e][:], (nj + e) % 2, range(NB), o_hi, o_lo)
                loop(pe, 1, NB // 2, out_tiles)

                nj = ffn_job(L)

                def in_tiles(i, first=False):
                    for e in range(2):
                        if not first:
                            pe.wait_ge(g_scaled, i * 2 + (L * NF + e - 1))
                        job_ready(nj + 2 * e, i * 4)
                        product(gate[e][:], nj % 2, range(NB), h_hi, h_lo, wait=h_ready(stage + 1) if first and e == 0 else None)
                        if first and e == 0:
                            sum_squares(stage + 1, False)
                        if not first:
                            pe.wait_ge(u_scaled, i * 2 + (L * NF + e - 1))
                        job_ready(nj + 2 * e + 1, i * 4)
                        product(up[e][:], (nj + 1) % 2, range(NB), h_hi, h_lo)
                in_tiles(0, first=True)
                loop(pe, 1, NF // 2, in_tiles)

                nj = ffn_out_job(L)
                fh = f_hi[:].rearrange("p (c t) -> p c t", c=NF)
                fl = f_lo[:].rearrange("p (c t) -> p c t", c=NF)

                def f_ready(k):
                    pe.wait_ge(f_hi_ready, L * NF + k + 1)
                    pe.wait_ge(f_lo_ready, L * NF + k + 1)

                def ffn_tiles(i, first=False):
                    for e in range(2):
                        if not first:
                            added(stage + 2, i, e)
                        for c, (a, b) in enumerate(OUT_CHUNKS):
                            k = NOUT * e + c
                            job_ready(nj + k, i * 6)
                            product(outs[e][:], (nj + k) % 2, range(a, b), fh, fl, c == 0, c == NOUT - 1,
                                    f_ready if first and e == 0 else None)
                ffn_tiles(0, first=True)
                loop(pe, 1, NB // 2, ffn_tiles)
            sum_squares(2 * DEPTH, False)

        @block.scalar
        def _(act):
            f = nc.scalar.activation

            def alone():
                nc.scalar.nop(nofuse=True)

            def split(n0, di=0, half=0, width=JOB, view=None):
                s = n0 % 2
                act.wait_ge(w_loaded[s], half * 16 + 16 * (n0 // 2 + 1))
                if n0 >= 2:
                    act.wait_ge(job_done, di + (n0 - 1))
                view = view or (lambda w: w[:, s, 0:width])
                f(view(w_hi), view(w_raw), ACT.Copy).then_inc(w_hi_ready, 1)

            def squares(stage, m, e, first=False):
                if not first:
                    act.wait_ge(ssq_ready, m + (stage * NB - 1))
                    alone()
                f((tmp, tmp2)[e][:], x[:, m if isinstance(m, slice) else blk(m), :], ACT.Square).then_inc(sq_ready, 1)

            def gained(stage, m, e):
                g = gains[:, stage, blk(m)]
                if stage < 2 * DEPTH:
                    f(h_hi[:, blk(m), :], x[:, blk(m), :], ACT.Copy, scale=g).then_inc(h_hi_ready, 1)
                else:
                    f(y32[:, blk(m), :], x[:, blk(m), :], ACT.Copy, scale=g).then_inc(h_hi_ready, 1)

            def inverse_rms(stage, cols, lns):
                act.wait_ge(ssq_summed, stage + 1)
                f(rms[:], sums[:], ACT.Ln, bias=eps[:], scale=1.0 / D).then_inc(ln_done, 1)
                if cols:
                    f(rms_col[:], col_sums[:, 0:NT], ACT.Ln, bias=eps[:], scale=1.0 / D).then_inc(ln_done, 1)
                    act.wait_ge(ln_done, lns + 2)
                    f(rms_col[:], rms_col[:], ACT.Exp, scale=-0.5)
                act.wait_ge(ln_done, lns + 1)
                f(rms[:], rms[:], ACT.Exp, scale=-0.5).then_inc(rms_raw, 1)

            def heads_out(S, e, at):
                act.wait_ge(o_summed, S + 1)
                alone()
                r = slice(DH * e, DH * (e + 1))
                f(o_hi[r, at, :], ob[r, :], ACT.Copy).then_inc(o_hi_ready, 1)

            def finish(kind, S, e):
                for n, b in enumerate(KR):
                    act.wait_ge(second_ready, S * SIGNALS + DONE[n])
                    c = slice(KO[b], KO[b] + KW[b])
                    if kind == "stick":
                        f(s32[e][:, c], zt(e, KW[b]), ACT.Exp).then_inc(stick_exp, 1)
                    else:
                        f(pt[e][0][:, c], zt(e, KW[b]), ACT.Copy).then_inc(pt_hi_ready, 1)

            def hi_part(to, x):
                return f(to, x, ACT.Copy)

            def pair(L, kind, j, before=None, splits=True, last=False):
                for e in range(2):
                    S = j * 2 + (L * HEADS + e)
                    buf = s32[e]
                    if before:
                        heads_out(S - 2, e, blk(j - 1))
                    if e == 1:
                        f(v_hi[:], v32[:, :, bass.ds(j * P, P)], ACT.Copy).then_inc(vs_hi_ready, 1)
                    if splits and kind != "stick":
                        split(first_qk_job(L) + 4 + e, j * 2, j)
                    if kind == "stick":
                        for n, b in enumerate(KR):
                            act.wait_ge(z_ready, S * SIGNALS + DONE[n])
                            f(buf[:, KO[b]:KO[b] + KW[b]], zt(e, KW[b]), ACT.Abs).then_inc(abs_ready, 1)
                    if before or e == 1:
                        finish(before if e == 0 else kind, S - 1, 1 - e)
                    if kind != "stick":
                        X = S - 2 * STICK
                        for n, b in enumerate(QR):
                            act.wait_ge(max_ready, X * NT + PASSED[n])
                            sums = {"accum_out": rsum[:, b:b + 1]} if kind == "fox" else {}
                            f(buf[:, QO[b]:QO[b] + QW[b]], zt(e, QW[b]), ACT.Exp,
                              bias=nmax[:, b:b + 1], **sums).then_inc(rows_exp, 1)
                    if splits and kind != "stick" and not (last and e == 1):
                        pieces(act, hi_part, None, None, L, kind, j + 1, range(1, 4) if e else range(1))
                    if splits and kind == "stick":
                        split(first_qk_job(L) + 4 + e, j * 2, j)
                    if kind == "dil":
                        for n, b in enumerate(QR):
                            act.wait_ge(rows_inv, X * NT + (n + 1))
                            c = slice(QO[b], QO[b] + QW[b])
                            f(buf[:, c], buf[:, c], ACT.Copy, scale=rinv[:, b:b + 1]).then_inc(rows_ready, 1)
                    if kind == "stick":
                        for n, b in enumerate(KR):
                            act.wait_ge(abs_ready, S * NT + (n + 1))
                            c = slice(KO[b], KO[b] + KW[b])
                            f(buf[:, c], buf[:, c], ACT.Exp, scale=-1.0).then_inc(exp_done, 1)
                        for n, b in enumerate(KR):
                            act.wait_ge(exp_done, S * NT + (n + 1))
                            c = slice(KO[b], KO[b] + KW[b])
                            f(buf[:, c], buf[:, c], ACT.Ln, bias=1.0).then_inc(ln_ready, 1)

            nc.scalar.preload_act_table_set("natural_log_exp_and_others")
            act.wait_ge(gains_loaded, 16)
            act.wait_ge(eps_ready, 1)
            for m in range(NB):
                act.wait_ge(x_loaded[[a <= m < b for a, b in X_LOADS].index(True)], 16)
                gained(0, m, m % 2)
                if m == 0:
                    act.wait_ge(start_loaded, 16)
                    f(w_hi[:, 0, 0:T], w_raw[:, 0, 0:T], ACT.Copy).then_inc(start_hi_ready, 1)
                elif m == 1:
                    split(0, view=second_half)
                elif m == 2:
                    split(1)
                squares(0, m, m % 2, first=m < 2)
            split(2)
            act.wait_ge(const_loaded, 16 * 5)
            act.wait_ge(ones_ready, 1)
            for dst, a, b in ((m_dil[:], 0, T), (m_causal[:], T, T + P), (m_strict[:], T + P, T + 2 * P),
                              (ident_b[:], T + 2 * P, T + 3 * P), (ident[:], T + 2 * P, T + 3 * P), (neg_tri, T + 3 * P, D)):
                f(dst, masks32[:, a:b], ACT.Copy).then_inc(const_ready, 1)
            f(neg_one, ones[:], ACT.Copy, scale=-1.0).then_inc(const_ready, 1)

            for L in range(DEPTH):
                stage = 2 * L
                n = JOB0[L] + L
                fq = first_qk_job(L)
                if L == 1:
                    nc.scalar.preload_act_table_set("natural_log_exp_and_others")
                    split(n)
                    split(n + 1)
                    inverse_rms(stage, True, 3 * L)
                    act.wait_ge(fg_step, 3)
                    f(fg_soft, fg_soft, ACT.Exp, scale=-1.0).then_inc(fg_act, 1)
                    act.wait_ge(fg_act, 1)
                    f(fg_soft, fg_soft, ACT.Ln, bias=1.0).then_inc(fg_act, 1)
                    split(n + 2)
                    f(tmp_r[0], fg_one, ACT.Copy).then_inc(fg_act, 1)
                    act.wait_ge(fg_step, 7)
                    f(tmp_r[3], tmp_r[1].bitcast(F32), ACT.Copy, scale=-1.0).then_inc(fg_act, 1)
                    f(tmp_r[4], tmp_r[2].bitcast(F32), ACT.Copy, scale=-1.0).then_inc(fg_act, 1)
                for c in range(2, JV):
                    if c != 4:
                        split(n + c + 1)
                    if c == 3:
                        if L == 0:
                            inverse_rms(stage, True, 0)
                        split(n + 5)
                    if c == 4:
                        act.wait_ge(col_ready, L + 1)
                        act.wait_ge(job_done, n + 4)
                        for t in range(NT):
                            f(v32[:, t, 0:T], vb[0][t][:], ACT.Copy, scale=rms_col[:, t:t + 1]).then_inc(v_ready, 1)
                act.wait_ge(job_done, n + JV)
                for t in range(NT):
                    f(v32[:, t, T:D], vb[1][t][:], ACT.Copy, scale=rms_col[:, t:t + 1]).then_inc(v_ready, 1)
                for t in range(1, 4):
                    split(fq + t)
                act.wait_ge(v_ready, (2 * L + 2) * NT)
                if L == 0:
                    pair(0, "stick", 0)
                    loop(act, 1, STICK, lambda j: pair(0, "stick", j, "stick"))
                    pair(0, "dil", STICK, "stick")
                    loop(act, STICK + 1, NPAIR - 2, lambda j: pair(0, "dil", j, "dil"))
                    pair(0, "dil", NPAIR - 2, "dil", last=True)
                    pair(0, "dil", NPAIR - 1, "dil", splits=False)
                else:
                    pair(1, "fox", 0)
                    loop(act, 1, NPAIR - 2, lambda j: pair(1, "fox", j, "fox"))
                    pair(1, "fox", NPAIR - 2, "fox", last=True)
                    pair(1, "fox", NPAIR - 1, "fox", splits=False)
                finish("fox", (L + 1) * HEADS - 1, 1)
                for e in range(2):
                    heads_out((L + 1) * HEADS - 2 + e, e, blk(NPAIR - 1))

                def tail(stage, m, e):
                    act.wait_ge(x_new, m + ((stage - 1) * NB + 1))
                    alone()
                    if stage == 2 * DEPTH:
                        squares(stage, m, e)
                    gained(stage, m, e)
                    if stage < 2 * DEPTH:
                        squares(stage, m, e)

                nj = out_job(L)

                def out_tiles(i):
                    for e in range(2):
                        split(nj + e + 2, i * 2, i)
                        tail(stage + 1, i * 2 + e, e)
                loop(act, 0, NB // 2, out_tiles)

                nj = ffn_job(L)

                def in_tile(i, first=False):
                    if not first:
                        split(nj + 1, i * 2, i)
                    else:
                        split(nj + 2)
                        inverse_rms(stage + 1, False, 3 * L + 2)
                        nc.scalar.preload_act_table_set("sigmoid_and_others")
                    act.wait_ge(g_scaled, i + (L * NF + 1))
                    f(f_sig, f_gate, ACT.Sigmoid).then_inc(g_sig, 1)
                    if not first:
                        split(nj + 2, i * 2, i)
                    act.wait_ge(act_ready, i + (L * NF + 1))
                    alone()
                    f(f_hi[:].rearrange("p (c t) -> p c t", c=NF)[:, blk(i), :], tmp[:], ACT.Copy).then_inc(f_hi_ready, 1)
                in_tile(0, first=True)
                loop(act, 1, NF, in_tile)

                nj = ffn_out_job(L)

                def ffn_tiles(i, last=False):
                    for e in range(2):
                        for c in range(NOUT):
                            k = NOUT * e + c + 1
                            if last and L == DEPTH - 1 and k == 2 * NOUT:
                                break
                            a, b = OUT_CHUNKS[k % NOUT]
                            if last and k == 2 * NOUT:
                                split(g_job, view=gate_cols)
                            else:
                                split(nj + k, i * 6, i * 3, (b - a) * P)
                        tail(stage + 2, i * 2 + e, e)
                loop(act, 0, NB // 2 - 1, ffn_tiles)
                ffn_tiles(NB // 2 - 1, last=True)
            nc.scalar.preload_act_table_set("natural_log_exp_and_others")
            inverse_rms(2 * DEPTH, False, 3 * DEPTH)

        @block.vector
        def _(dve):
            v = nc.vector

            def split(n0, di=0, width=JOB, view=None):
                s = n0 % 2
                dve.wait_ge(w_hi_ready, di + (n0 + 1))
                view = view or (lambda w: w[:, s, 0:width])
                v.tensor_tensor(view(w_lo), view(w_raw), view(w_hi).bitcast(F32), ALU.subtract).then_inc(w_lo_ready, 1)

            def gained(stage, m):
                dve.wait_ge(h_hi_ready, m + (stage * NB + 1))
                v.scalar_tensor_tensor(h_lo[:, blk(m), :], x[:, blk(m), :], gains[:, stage, blk(m)],
                                       h_hi[:, blk(m), :].bitcast(F32), ALU.mult, ALU.subtract).then_inc(h_lo_ready, 1)

            def refine(stage, cols):
                dve.wait_ge(rms_raw, stage + 1)
                done = [newtons[0]]

                def step(ins):
                    done[0] += 1
                    ins.then_inc(newton, 1)
                    dve.wait_ge(newton, done[0])

                def steps(y, sums, t):
                    step(v.tensor_tensor(t, y, y, ALU.mult))
                    step(v.scalar_tensor_tensor(t, sums, D * EPS, t, ALU.add, ALU.mult))
                    step(v.tensor_scalar(t, t, -0.5 / D, 1.5, ALU.mult, ALU.add))
                    return v.tensor_tensor(y, y, t, ALU.mult)
                if cols:
                    steps(rms_col[:], col_sums[:, 0:NT], col_tmp[:]).then_inc(col_ready, 1)
                steps(rms[:], sums[:], tmp3[:]).then_inc(rms_ready, 1)
                newtons[0] = done[0]
                dve.wait_ge(rms_ready, stage + 1)

            newtons = [0]

            def scaled(L, kind, j, e, src=pb, alone=True):
                dve.wait_ge(job_done, j * 2 + (first_qk_job(L) + e + 1))
                sc, to = ((SCALE, tmp), (1.0, tmp2))[e]
                if kind == "dil":
                    r = (j - STICK) * 2 + e
                    v.scalar_tensor_tensor(to[:], src[:], sc, cosr[:], ALU.mult, ALU.mult)
                    v.stream_shuffle(tmp3[:], src[:], SWAP).then_inc(rope_shuffled, 1)
                    if alone:
                        dve.wait_ge(rope_shuffled, r + 1)
                        v.scalar_tensor_tensor(tmp3[:], tmp3[:], sc, sinr[:], ALU.mult, ALU.mult).then_inc(rope_sin, 1)
                        dve.wait_ge(rope_sin, r + 1)
                        v.tensor_tensor(to[:], to[:], tmp3[:], ALU.add).then_inc(qk_scaled, 1)
                else:
                    v.scalar_tensor_tensor(to[:], src[:], sc, rms[:], ALU.mult, ALU.mult).then_inc(qk_scaled, 1)

            def lo_part(to, x, hi):
                return v.tensor_tensor(to, x, hi, ALU.subtract)

            def heads_out(S, e, at):
                dve.wait_ge(o_hi_ready, S + 1)
                r = slice(DH * e, DH * (e + 1))
                v.tensor_tensor(o_lo[r, at, :], ob[r, :], o_hi[r, at, :].bitcast(F32), ALU.subtract).then_inc(o_lo_ready, 1)

            def finish(kind, S, e):
                for n, b in enumerate(KR):
                    c = slice(KO[b], KO[b] + KW[b])
                    hi, lo = pt[e]
                    if kind == "stick":
                        dve.wait_ge(stick_exp, S * NT + (n + 1))
                        v.tensor_copy(hi[:, c], s32[e][:, c]).then_inc(a_hi_ready, 1)
                    else:
                        dve.wait_ge(pt_hi_ready, (S - 2 * STICK) * NT + PASSED[n])
                        v.tensor_tensor(lo[:, c], zt(e, KW[b]), hi[:, c].bitcast(F32), ALU.subtract).then_inc(pt_lo_ready, 1)

            def pair(L, kind, j, next_kind, before=None, splits=True, last=False):
                for e in range(2):
                    S = j * 2 + (L * HEADS + e)
                    X = S - 2 * STICK
                    buf = s32[e]
                    if next_kind:
                        dve.wait_ge(qk_lo_ready, j * 4 + (4 * L * NPAIR + 4))
                        if next_kind == kind == "dil":
                            dve.wait_ge(qk_scaled, j * 2 + (2 + e))
                        scaled(L, next_kind, j + 1, e, alone=kind == "stick")
                    if before:
                        heads_out(S - 2, e, blk(j - 1))
                    if e == 1:
                        dve.wait_ge(vs_hi_ready, j + (L * NPAIR + 1))
                        v.tensor_tensor(v_lo[:], v32[:, :, bass.ds(j * P, P)], v_hi[:].bitcast(F32), ALU.subtract).then_inc(vs_ready, 1)
                    if last and e == 1:
                        pieces(dve, v.tensor_copy, None, None, L, next_kind, j + 1, range(1, 4))
                    if kind != "stick":
                        for n, b in enumerate(QR):
                            dve.wait_ge(z_ready, S * SIGNALS + DONE[n])
                            v.tensor_reduce(nmax[:, b:b + 1], zt(e, QW[b]), AX, ALU.max, negate=True).then_inc(max_ready, 1)
                    if kind == "stick":
                        pieces(dve, v.tensor_copy, lo_part, v.tensor_copy, L, next_kind, j + 1, range(1, 4) if e else range(1))
                    if before or e == 1:
                        finish(before if e == 0 else kind, S - 1, 1 - e)
                    if kind != "stick" and next_kind:
                        pieces(dve, None, None, v.tensor_copy, L, next_kind, j + 1, range(1, 4) if e else range(1))
                    if splits and kind == "stick":
                        split(first_qk_job(L) + 4 + e, j * 2)
                    if kind == "stick":
                        if before or e == 1:
                            dve.wait_ge(second_ready, S * SIGNALS)

                        def high(n):
                            b = KR[n]
                            dve.wait_ge(sp_ready, S * NT + (n + 1))
                            c = slice(KO[b], KO[b] + KW[b])
                            v.tensor_copy(sp_hi[:, c], buf[:, c]).then_inc(sp_hi_ready, 1)
                        for n, b in enumerate(KR):
                            dve.wait_ge(ln_ready, S * NT + (n + 1))
                            c = slice(KO[b], KO[b] + KW[b])
                            v.scalar_tensor_tensor(buf[:, c], zt(e, KW[b]), 0.0, buf[:, c], ALU.max, ALU.add).then_inc(sp_ready, 1)
                            if n:
                                high(n - 1)
                        high(NT - 1)
                    else:
                        def inverse(n):
                            b = QR[n]
                            v.reciprocal(rinv[:, b:b + 1], rsum[:, b:b + 1]).then_inc(rows_inv, 1)

                        def normalised(n):
                            b = QR[n]
                            dve.wait_ge(rows_inv, X * NT + (n + 1))
                            c = slice(QO[b], QO[b] + QW[b])
                            v.tensor_scalar(buf[:, c], buf[:, c], rinv[:, b:b + 1], None, ALU.mult).then_inc(rows_ready, 1)

                        for n, b in enumerate(QR):
                            dve.wait_ge(rows_exp, X * NT + (n + 1))
                            c = slice(QO[b], QO[b] + QW[b])
                            if kind == "dil":
                                v.scalar_tensor_tensor(buf[:, c], buf[:, c], 1.0, mult[:, T - QW[b]:T], ALU.mult, ALU.mult,
                                                       accum_out=rsum[:, b:b + 1]).then_inc(rows_mult, 1)
                                if n:
                                    dve.wait_ge(rows_mult, X * NT + n)
                                    inverse(n - 1)
                            else:
                                inverse(n)
                                if n:
                                    normalised(n - 1)
                        if kind == "dil":
                            dve.wait_ge(rows_mult, X * NT + NT)
                            inverse(NT - 1)
                        else:
                            normalised(NT - 1)

            v.memset(eps[:], EPS).then_inc(eps_ready, 1)
            for e in range(2):
                last = v.memset(mv2[e][other(e), :].bitcast(F32), 0.0)
            last.then_inc(mv2_clear, 1)
            v.memset(ones[:], 1.0).then_inc(ones_ready, 1)
            dve.wait_ge(gains_loaded, 16)
            for m in range(NB):
                gained(0, m)
                if m == 0:
                    dve.wait_ge(start_hi_ready, 1)
                    v.tensor_tensor(w_lo[:, 0, 0:T], w_raw[:, 0, 0:T], w_hi[:, 0, 0:T].bitcast(F32),
                                    ALU.subtract).then_inc(start_lo_ready, 1)
                elif m == 1:
                    split(0, view=second_half)
                elif m == 2:
                    split(1)
            for L in range(DEPTH):
                stage = 2 * L
                n = JOB0[L] + L
                fq = first_qk_job(L)
                if L == 1:
                    v.memset(fg_one, 1.0).then_inc(ones_ready, 1)
                    split(n)
                    split(n + 1)
                    refine(stage, True)
                    dve.wait_ge(job_done, g_job + 1)
                    v.tensor_tensor(fg_z, logits[0:HEADS, :], rms[0:HEADS, :], ALU.mult).then_inc(fg_step, 1)
                    dve.wait_ge(fg_step, 1)
                    v.tensor_scalar(fg_z, fg_z, bforget[:], None, ALU.add).then_inc(fg_step, 1)
                    dve.wait_ge(fg_step, 2)
                    v.scalar_tensor_tensor(fg_soft, fg_z, -1.0, fg_z, ALU.mult, ALU.max).then_inc(fg_step, 1)
                    dve.wait_ge(fg_act, 2)
                    v.scalar_tensor_tensor(fg_z, fg_z, 0.0, fg_soft, ALU.min, ALU.subtract).then_inc(fg_step, 1)
                    split(n + 2)
                    dve.wait_ge(fg_step, 4)
                    v.tensor_tensor_scan(fg_sum, fg_one, fg_z, 0.0, ALU.mult, ALU.add).then_inc(fg_step, 1)
                    dve.wait_ge(fg_step, 5)
                    v.tensor_copy(tmp_r[1], fg_sum).then_inc(fg_step, 1)
                    dve.wait_ge(fg_step, 6)
                    v.tensor_tensor(tmp_r[2], fg_sum, tmp_r[1].bitcast(F32), ALU.subtract).then_inc(fg_step, 1)
                for c in range(1 + L, JV):
                    if c != 4:
                        split(n + c + 1)
                    if c == 3:
                        if L == 0:
                            refine(stage, True)
                        split(n + 5)
                    if c == 4 and L == 0:
                        dve.wait_ge(const_loaded, 16 * 5)
                        v.tensor_tensor(cosr[:], cosr[:], rms[:], ALU.mult).then_inc(rope_ready, 1)
                        v.tensor_tensor(sinr[:], sinr[:], rms[:], ALU.mult).then_inc(rope_ready, 1)
                        dve.wait_ge(rope_ready, 2)
                        v.tensor_scalar(sin_q, sinr[:], SCALE, None, ALU.mult).then_inc(rope_ready, 1)
                kind = ("stick", "fox")[L]
                split(fq + 1)
                scaled(L, kind, 0, 0, src=first_tiles[0])
                split(fq + 2)
                scaled(L, kind, 0, 1, src=first_tiles[1])
                pieces(dve, v.tensor_copy, lo_part, v.tensor_copy, L, kind, 0, range(4))
                split(fq + 3)
                if L == 0:
                    pair(0, "stick", 0, "stick")
                    loop(dve, 1, STICK - 1, lambda j: pair(0, "stick", j, "stick", "stick"))
                    pair(0, "stick", STICK - 1, "dil", "stick")
                    pair(0, "dil", STICK, "dil", "stick")
                    loop(dve, STICK + 1, NPAIR - 2, lambda j: pair(0, "dil", j, "dil", "dil"))
                    pair(0, "dil", NPAIR - 2, "dil", "dil", last=True)
                    pair(0, "dil", NPAIR - 1, None, "dil", splits=False)
                else:
                    pair(1, "fox", 0, "fox")
                    loop(dve, 1, NPAIR - 2, lambda j: pair(1, "fox", j, "fox", "fox"))
                    pair(1, "fox", NPAIR - 2, "fox", "fox", last=True)
                    pair(1, "fox", NPAIR - 1, None, "fox", splits=False)
                finish("fox", (L + 1) * HEADS - 1, 1)
                for e in range(2):
                    heads_out((L + 1) * HEADS - 2 + e, e, blk(NPAIR - 1))

                def tail(stage, m, e, done, di, between=None):
                    dve.wait_ge(job_done, di + (done + 1))
                    v.tensor_tensor(x[:, blk(m), :], x[:, blk(m), :], outs[e][:], ALU.add).then_inc(x_new, 1)
                    if between:
                        between()
                    if stage < 2 * DEPTH:
                        gained(stage, m)

                nj = out_job(L)

                def out_tiles(i, first=False):
                    for e in range(2):
                        if first and e == 0:
                            dve.wait_ge(w_lo_ready, nj + 2)
                        tail(stage + 1, i * 2 + e, e, nj + e, i * 2, lambda: split(nj + e + 2, i * 2))
                out_tiles(0, first=True)
                loop(dve, 1, NB // 2, out_tiles)

                nj = ffn_job(L)

                def in_tile(i, e, first=False):
                    t = i + L * NF
                    if not first:
                        split(nj + 1, i * 2)
                    else:
                        split(nj + 2)
                        refine(stage + 1, False)
                    dve.wait_ge(job_done, i * 2 + (nj + 1))
                    v.tensor_tensor(f_gate, gate[e][:], rms[:], ALU.mult).then_inc(g_scaled, 1)
                    if not first:
                        split(nj + 2, i * 2)
                    dve.wait_ge(g_sig, t + 1)
                    v.tensor_tensor(f_silu, f_gate, f_sig, ALU.mult).then_inc(g_silu, 1)
                    dve.wait_ge(job_done, i * 2 + (nj + 2))
                    v.tensor_tensor(f_up, up[e][:], rms[:], ALU.mult).then_inc(u_scaled, 1)
                    dve.wait_ge(u_scaled, t + 1)
                    if not (first and L == 0):
                        dve.wait_ge(f_lo_ready, t)
                    v.tensor_tensor(tmp[:], f_silu, f_up, ALU.mult).then_inc(act_ready, 1)
                    dve.wait_ge(f_hi_ready, t + 1)
                    v.tensor_tensor(f_lo[:].rearrange("p (c t) -> p c t", c=NF)[:, blk(i), :], tmp[:],
                                    f_hi[:].rearrange("p (c t) -> p c t", c=NF)[:, blk(i), :].bitcast(F32),
                                    ALU.subtract).then_inc(f_lo_ready, 1)
                in_tile(0, 0, first=True)
                in_tile(1, 1)

                def in_tiles(i):
                    for e in range(2):
                        in_tile(i * 2 + e, e)
                loop(dve, 1, NF // 2, in_tiles)

                nj = ffn_out_job(L)

                def ffn_tiles(i, last=False):
                    for e in range(2):
                        for c in range(NOUT):
                            k = NOUT * e + c + 1
                            if last and L == DEPTH - 1 and k == 2 * NOUT:
                                break
                            a, b = OUT_CHUNKS[k % NOUT]
                            if last and k == 2 * NOUT:
                                split(g_job, view=gate_cols)
                            else:
                                split(nj + k, i * 6, (b - a) * P)
                        tail(stage + 2, i * 2 + e, e, nj + NOUT * e + 2, i * 6)
                loop(dve, 0, NB // 2 - 1, ffn_tiles)
                ffn_tiles(NB // 2 - 1, last=True)
            refine(2 * DEPTH, False)
            for m in range(NB - POOL_OUT):
                v.tensor_tensor(y32[:, m, :], y32[:, m, :], rms[:], ALU.mult).then_inc(out_ready, 1)

        @block.gpsimd
        def _(pool):
            g = nc.gpsimd

            def squares(stage, m, e, first=False):
                pool.wait_ge(sq_ready, m + (stage * NB + 1))
                sq = (tmp, tmp2)[e][:]
                if first:
                    if stage:
                        pool.wait_ge(ssq_summed, stage)
                    g.tensor_copy(ssq[:], sq).then_inc(ssq_ready, 1)
                else:
                    pool.wait_ge(ssq_ready, m + stage * NB)
                    g.tensor_tensor(ssq[:], ssq[:], sq, ALU.add).then_inc(ssq_ready, 1)

            def stage_squares(stage):
                def two(i, first=False):
                    for e in range(2):
                        squares(stage, i * 2 + e, e, first and e == 0)
                two(0, first=True)
                loop(pool, 1, NB // 2, two)

            def low(S, e, ready, hi, lo, done):
                for n, b in enumerate(KR):
                    pool.wait_ge(ready, S * NT + (n + 1))
                    c = slice(KO[b], KO[b] + KW[b])
                    g.tensor_tensor(lo[:, c], s32[e][:, c], hi[:, c].bitcast(F32), ALU.subtract).then_inc(done, 1)

            def weights(S, e):
                low(S, e, a_hi_ready, *pt[e], a_lo_ready)

            def stick_pair(j, first=False):
                for e in range(2):
                    S = j * 2 + e
                    if not (first and e == 0):
                        weights(S - 1, 1 - e)
                    low(S, e, sp_hi_ready, sp_hi, sp_lo, sp_lo_ready)

            def lo_part(to, x, hi):
                return g.tensor_tensor(to, x, hi, ALU.subtract)

            def softmax_pair(L, kind, j, finish=False):
                for e in range(2):
                    if kind == "dil":
                        r = (j - STICK) * 2 + (2 + e)
                        pool.wait_ge(rope_shuffled, r + 1)
                        g.tensor_tensor(tmp3[:], tmp3[:], (sin_q, sinr[:])[e], ALU.mult).then_inc(rope_sin, 1)
                        pool.wait_ge(rope_sin, r + 1)
                        to = (tmp, tmp2)[e]
                        g.tensor_tensor(to[:], to[:], tmp3[:], ALU.add).then_inc(qk_scaled, 1)
                        pool.wait_ge(qk_scaled, j * 2 + (3 + e))
                    n0 = first_qk_job(L) + 4 + e
                    s = n0 % 2
                    pool.wait_ge(w_hi_ready, j * 2 + (n0 + 1))
                    pool.wait_ge(w_lo_ready, j * 2 + n0)
                    g.tensor_tensor(w_lo[:, s], w_raw[:, s], w_hi[:, s].bitcast(F32), ALU.subtract).then_inc(w_lo_ready, 1)
                    pool.wait_ge(w_lo_ready, j * 2 + (n0 + 1))
                    if finish and e == 0:
                        weights(2 * STICK - 1, 1)
                        pool.wait_ge(a_lo_ready, 2 * STICK * NT)
                    for i in (range(1, 4) if e else range(1)):
                        if i:
                            pool.wait_ge(qk_lo_ready, j * 4 + (4 * L * NPAIR + 4 + i))
                        pieces(pool, None, lo_part, None, L, kind, j + 1, range(i, i + 1))
                    pool.wait_ge(qk_lo_ready, j * 4 + (4 * L * NPAIR + 5 + (3 if e else 0)))

            stage_squares(0)
            stick_pair(0, first=True)
            loop(pool, 1, STICK, stick_pair)
            pool.wait_ge(rope_ready, 3)
            softmax_pair(0, "dil", STICK, finish=True)
            loop(pool, STICK + 1, NPAIR - 1, lambda j: softmax_pair(0, "dil", j))
            for stage in range(1, 2 * DEPTH + 1):
                stage_squares(stage)
                if stage == 2:
                    pool.wait_ge(job_done, JOB0[1])
                    pool.wait_ge(ssq_ready, 3 * NB)
                    for side, rows in enumerate((st2[0], mv2[0], st2[1], mv2[1])):
                        if side == 2:
                            pool.wait_ge(rows_clear, 2)
                        g.memset(rows[other(side // 2), :].bitcast(F32), 0.0).then_inc(rows_clear, 1)
                    pool.wait_ge(rows_clear, 4)
                    loop(pool, 0, NPAIR - 1, lambda j: softmax_pair(1, "fox", j))

            pool.wait_ge(rms_ready, 2 * DEPTH + 1)
            for m in range(NB - POOL_OUT, NB):
                g.tensor_tensor(y32[:, m, :], y32[:, m, :], rms[:], ALU.mult).then_inc(pool_out_ready, 1)


def _tables():
    q = np.arange(P)[:, None]
    k = np.arange(T)[None, :] - (T - P)
    dist = q - k
    mult = ((dist >= 0) & (dist <= 128)).astype(np.float32)
    mult += (dist >= 0) & (dist % 4 == 0)
    mult += (dist >= 0) & (dist % 16 == 0)
    dil = np.where(mult > 0, 0.0, MASKED)
    r = np.arange(P)
    causal = np.where(r[None, :] <= r[:, None], 0.0, MASKED)
    strict = np.where(r[:, None] < r[None, :], 0.0, MASKED)
    tri = np.where(r[:, None] >= r[None, :], -1.0, 0.0)
    masks = np.concatenate([dil, causal, strict, np.eye(P), tri], 1).astype(np.float32)
    half = ROT // 2
    inv = (np.float32(THETA) ** (-np.arange(half, dtype=np.float32) * np.float32(2.0) / np.float32(ROT))).astype(np.float32)
    ang = np.arange(T, dtype=np.float32)[None, :] * inv[:, None]
    cos, sin = np.cos(ang), np.sin(ang)
    rope = np.zeros((2, P, T), np.float32)
    rope[0] = 1.0
    for h in (0, DH):
        rope[0, h:h + half] = rope[0, h + half:h + ROT] = cos
        rope[1, h:h + half], rope[1, h + half:h + ROT] = -sin, sin
    return rope, mult.astype(np.float32), masks


def _tiles(w):
    k, n = w.shape
    return w.reshape(k // P, P, n // P, P).transpose(2, 1, 0, 3).reshape(n // P, P, k)


def _attention_jobs(w, w_o):
    q, k, v = w[:, 0:D], w[:, D:2 * D], w[:, 2 * D:3 * D]
    vj = v.reshape(4, 2, P, 2, T).transpose(3, 0, 2, 1, 4).reshape(JV, P, JOB)
    qk = np.stack([_tiles(q), _tiles(k)], 1).reshape(JQK, P, JOB)
    return np.ascontiguousarray(np.concatenate([vj, qk, _tiles(w_o)], 0))


def kernel(x, norm_mix, w_qkv_even, w_o_even, w_qkvf_odd, b_forget, w_o_odd, norm_ffn, w_ffn_in, w_ffn_out, norm_final):
    import concourse.bacc as _bacc
    from concourse.bass_utils import run_bass_kernel_spmd as _run

    a = np.asarray
    xt = a(x)[0].T.reshape(NB, P, T).transpose(1, 0, 2)
    gains = np.stack([a(norm_mix)[0], a(norm_ffn)[0], a(norm_mix)[1], a(norm_ffn)[1], a(norm_final)], 0)
    wf = a(w_qkvf_odd)[0][:, 3 * D:].reshape(NB, P, HEADS).transpose(1, 0, 2)
    win = np.stack([np.stack([_tiles(w[:, :DFF]), _tiles(w[:, DFF:])], 1).reshape(JIN, P, D) for w in a(w_ffn_in)])
    wout = np.stack([_tiles(w) for w in a(w_ffn_out)])
    rope, mult, masks = _tables()
    arrays = {
        "xt": xt, "gains": gains.reshape(2 * DEPTH + 1, NB, P).transpose(2, 0, 1),
        "wa0": _attention_jobs(a(w_qkv_even)[0], a(w_o_even)[0]),
        "wa1": _attention_jobs(a(w_qkvf_odd)[0], a(w_o_odd)[0]),
        "wf": wf, "win": win, "wout": wout, "bf": a(b_forget)[0][:, None],
        "rope": rope, "mult": mult, "masks": masks,
    }
    nc = _bacc.Bacc("TRN2", target_bir_lowering=False, num_devices=1)
    feed, args = {}, []
    for name, v in arrays.items():
        v = np.ascontiguousarray(v)
        feed[f"in_{name}"] = v
        args.append(nc.dram_tensor(f"in_{name}", v.shape, mybir.dt.from_np(v.dtype), kind="ExternalInput").ap())
    args.append(nc.dram_tensor("out_t", (P, NB, T), F32, kind="ExternalOutput").ap())
    trunk(nc, *args)
    r = _run(nc, [feed], core_ids=[0])
    out = r.results[0]["out_t"]
    return np.ascontiguousarray(out.transpose(2, 1, 0).reshape(T, D))[None]
```
